# Optimizing a Trainium2 kernel written in Bass

```python
import jax
import jax.numpy as jnp
from jax import lax
import numpy as np

D_MODEL = 1024
BATCH = 1
SEQ = 512
DEPTH = 1

CHUNK = 64
EPS = 1e-6
NEG_INF = -1e30
CONV_CH = 512
CONV_K = 31
N_Q_HEADS = 8
N_KV_HEADS = 2
HEAD_DIM = 64
Q_GROUP = N_Q_HEADS // N_KV_HEADS
ATTN_WIDTH = N_Q_HEADS * HEAD_DIM
KV_WIDTH = N_KV_HEADS * HEAD_DIM
WINDOW = 128
WINDOW_CHUNKS = WINDOW // CHUNK
BAND = WINDOW_CHUNKS * CHUNK
N_BRANCH = 2
OFF_CONV = 0
OFF_Q = OFF_CONV + 2 * CONV_CH
OFF_K = OFF_Q + ATTN_WIDTH
OFF_V = OFF_K + KV_WIDTH
OFF_GATE = OFF_V + KV_WIDTH
IN_COLS = OFF_GATE + N_BRANCH * D_MODEL
PEER_HEADS = 8
PEER_NKEYS = 128
PEER_N = PEER_NKEYS * PEER_NKEYS
PEER_QDIM = 256
PEER_HALF = PEER_QDIM // 2
PEER_TOPK = 16
PEER_BLOCK = 128
N_MOD = 6

kernel_name = "hybrid_conv_swa_peer_block"

def rms_norm(x, g):
    x32 = x.astype(jnp.float32)
    y = x32 * lax.rsqrt(jnp.mean(x32 * x32, axis=-1, keepdims=True) + EPS)
    return (y * g.astype(jnp.float32)).astype(x.dtype)

def layer_norm(x, g, b):
    x32 = x.astype(jnp.float32)
    mu = jnp.mean(x32, axis=-1, keepdims=True)
    var = jnp.mean(jnp.square(x32 - mu), axis=-1, keepdims=True)
    y = (x32 - mu) * lax.rsqrt(var + EPS)
    return (y * g.astype(jnp.float32) + b.astype(jnp.float32)).astype(x.dtype)

def alibi_slopes(n):
    return jnp.asarray(2.0 ** (-8.0 * np.arange(1, n + 1) / n), dtype=jnp.float32)

def conformer_conv(a, w_dw, b_dw, ln_g, ln_b, w_pw):
    u = a[..., :CONV_CH] * jax.nn.sigmoid(a[..., CONV_CH:])
    y = lax.conv_general_dilated(
        u, w_dw[:, None, :].astype(u.dtype), window_strides=(1,),
        padding=[(CONV_K - 1, 0)],
        dimension_numbers=("NWC", "WIO", "NWC"), feature_group_count=CONV_CH)
    y = layer_norm(y + b_dw, ln_g, ln_b)
    return jax.nn.silu(y) @ w_pw

def _band(t):
    n_chunks = t.shape[1]
    tp = jnp.pad(t, ((0, 0), (WINDOW_CHUNKS - 1, 0), (0, 0), (0, 0), (0, 0)))
    return jnp.concatenate([tp[:, w:w + n_chunks] for w in range(WINDOW_CHUNKS)], axis=2)

def window_attention(q, k, v, sinks):
    b, s, _ = q.shape
    n_chunks = s // CHUNK
    q = q.reshape(b, n_chunks, CHUNK, N_KV_HEADS, Q_GROUP, HEAD_DIM) * (HEAD_DIM ** -0.5)
    kb = _band(k.reshape(b, n_chunks, CHUNK, N_KV_HEADS, HEAD_DIM))
    vb = _band(v.reshape(b, n_chunks, CHUNK, N_KV_HEADS, HEAD_DIM))
    scores = jnp.einsum("bcqkgd,bcjkd->bkgcqj", q, kb).astype(jnp.float32)
    qi = jnp.arange(CHUNK)[:, None]
    j = jnp.arange(BAND)[None, :]
    dist = jnp.abs(qi + (WINDOW_CHUNKS - 1) * CHUNK - j).astype(jnp.float32)
    valid = (jnp.arange(n_chunks)[:, None] + j // CHUNK - (WINDOW_CHUNKS - 1)) >= 0
    slopes = alibi_slopes(N_Q_HEADS).reshape(N_KV_HEADS, Q_GROUP)
    scores = scores - slopes[:, :, None, None, None] * dist
    scores = jnp.where(valid[:, None, :], scores, NEG_INF)
    sink = sinks.astype(jnp.float32).reshape(N_KV_HEADS, Q_GROUP)[None, :, :, None, None, None]
    m = jnp.maximum(jnp.max(scores, axis=-1, keepdims=True), sink)
    p = jnp.exp(scores - m)
    p = p / (jnp.sum(p, axis=-1, keepdims=True) + jnp.exp(sink - m))
    o = jnp.einsum("bkgcqj,bcjkd->bcqkgd", p.astype(vb.dtype), vb)
    return o.reshape(b, s, ATTN_WIDTH)

def peer(xn, w_pq, sub_keys, u, v):
    b, s, d = xn.shape
    t = b * s
    xf = xn.reshape(t, d)
    q = (xf @ w_pq).reshape(t, PEER_HEADS, 2, PEER_HALF)
    sc = jnp.einsum("thpd,hpnd->thpn", q, sub_keys).astype(jnp.float32)
    vals, idx = lax.top_k(sc, PEER_TOPK)
    cand = (vals[:, :, 0, :, None] + vals[:, :, 1, None, :]).reshape(t, PEER_HEADS, PEER_TOPK * PEER_TOPK)
    cidx = (idx[:, :, 0, :, None] * PEER_NKEYS + idx[:, :, 1, None, :]).reshape(t, PEER_HEADS, PEER_TOPK * PEER_TOPK)
    best, pos = lax.top_k(cand, PEER_TOPK)
    eidx = jnp.take_along_axis(cidx, pos, axis=-1)
    g = jax.nn.softmax(best, axis=-1).astype(xn.dtype)
    n_blk = t // PEER_BLOCK
    eidx = eidx.reshape(n_blk, PEER_BLOCK, PEER_HEADS * PEER_TOPK)
    g = g.reshape(n_blk, PEER_BLOCK, PEER_HEADS * PEER_TOPK)
    xb = xf.reshape(n_blk, PEER_BLOCK, d)

    def block(args):
        xt, it, gt = args
        ue = jnp.take(u, it, axis=0)
        act = jax.nn.gelu(jnp.einsum("td,tkd->tk", xt, ue), approximate=False) * gt
        ve = jnp.take(v, it, axis=0)
        return jnp.einsum("tk,tkd->td", act, ve)

    out = lax.map(block, (xb, eidx, g))
    return out.reshape(b, s, d)

def setup_inputs(seed: int = 0) -> dict:
    key = jax.random.key(seed)
    ks = jax.random.split(key, 24)
    f32 = jnp.float32
    nrm = lambda k, shape, sc: jax.random.normal(k, shape, f32) * sc
    return {
        "x": nrm(ks[0], (BATCH, SEQ, D_MODEL), 1.0),
        "c": nrm(ks[1], (BATCH, D_MODEL), 1.0),
        "w_ada": nrm(ks[2], (DEPTH, D_MODEL, N_MOD * D_MODEL), D_MODEL ** -0.5),
        "b_ada": nrm(ks[3], (DEPTH, N_MOD * D_MODEL), 0.02),
        "g_norm1": 1.0 + nrm(ks[4], (DEPTH, D_MODEL), 0.02),
        "w_in": nrm(ks[5], (DEPTH, D_MODEL, IN_COLS), D_MODEL ** -0.5),
        "w_dw": nrm(ks[6], (DEPTH, CONV_K, CONV_CH), CONV_K ** -0.5),
        "b_dw": nrm(ks[7], (DEPTH, CONV_CH), 0.02),
        "ln_g": 1.0 + nrm(ks[8], (DEPTH, CONV_CH), 0.02),
        "ln_b": nrm(ks[9], (DEPTH, CONV_CH), 0.02),
        "w_conv_out": nrm(ks[10], (DEPTH, CONV_CH, D_MODEL), CONV_CH ** -0.5),
        "w_attn_out": nrm(ks[11], (DEPTH, ATTN_WIDTH, D_MODEL), ATTN_WIDTH ** -0.5),
        "attn_sinks": nrm(ks[12], (DEPTH, N_Q_HEADS), 0.5),
        "w_out": nrm(ks[13], (DEPTH, D_MODEL, D_MODEL), D_MODEL ** -0.5),
        "g_norm2": 1.0 + nrm(ks[14], (DEPTH, D_MODEL), 0.02),
        "w_pq": nrm(ks[15], (DEPTH, D_MODEL, PEER_HEADS * PEER_QDIM), D_MODEL ** -0.5),
        "sub_keys": nrm(ks[16], (DEPTH, PEER_HEADS, 2, PEER_NKEYS, PEER_HALF), PEER_HALF ** -0.5),
        "peer_u": nrm(ks[17], (DEPTH, PEER_N, D_MODEL), D_MODEL ** -0.5),
        "peer_v": nrm(ks[18], (DEPTH, PEER_N, D_MODEL), PEER_TOPK ** -0.5),
        "g_final": 1.0 + nrm(ks[19], (D_MODEL,), 0.02),
    }

def reference(x, c, w_ada, b_ada, g_norm1, w_in, w_dw, b_dw, ln_g, ln_b, w_conv_out, w_attn_out,
              attn_sinks, w_out, g_norm2, w_pq, sub_keys, peer_u, peer_v, g_final):
    cond = jax.nn.silu(c)
    h = x
    for l in range(DEPTH):
        mod = (cond @ w_ada[l] + b_ada[l])[:, None, :]
        shift1, scale1, gate1, shift2, scale2, gate2 = jnp.split(mod, N_MOD, axis=-1)
        n1 = rms_norm(h, g_norm1[l]) * (1 + scale1) + shift1
        z = n1 @ w_in[l]
        branch_a = conformer_conv(z[..., OFF_CONV:OFF_Q], w_dw[l], b_dw[l], ln_g[l], ln_b[l], w_conv_out[l])
        attn = window_attention(z[..., OFF_Q:OFF_K], z[..., OFF_K:OFF_V], z[..., OFF_V:OFF_GATE], attn_sinks[l])
        branch_b = attn @ w_attn_out[l]
        gates = jax.nn.sigmoid(z[..., OFF_GATE:])
        merged = gates[..., :D_MODEL] * branch_a + gates[..., D_MODEL:] * branch_b
        h = h + gate1 * (merged @ w_out[l])
        n2 = rms_norm(h, g_norm2[l]) * (1 + scale2) + shift2
        h = h + gate2 * peer(n2, w_pq[l], sub_keys[l], peer_u[l], peer_v[l])
    return rms_norm(h, g_final)


_drawn_inputs = setup_inputs


def setup_inputs(seed=0):
    import zlib

    import numpy as np

    out = dict(_drawn_inputs(seed))
    spreads = {}
    factors = {'b_ada': 2.745,
     'g_norm1': 5.462,
     'b_dw': 6.081,
     'ln_g': 27.589,
     'ln_b': 27.118,
     'attn_sinks': 8.0,
     'g_norm2': 16.569,
     'g_final': 7.839}
    for name, (base, spread) in spreads.items():
        noise = np.random.default_rng([zlib.crc32(name.encode()), seed]).standard_normal(out[name].shape)
        drawn = base * np.exp(spread * noise) if base else spread * noise
        out[name] = jnp.asarray(drawn.astype(out[name].dtype))
    for name, factor in factors.items():
        out[name] = (out[name] * factor).astype(out[name].dtype)
    return out
```

```python
import math

import numpy as np
import concourse.bass as bass
from concourse import mybir
from contextlib import ExitStack

P = 128
D = 1024
T = 512
KT = D // P
TB = T // P
CT = 4
TAPS = 31
HEADS = 8
HD = 64
PAIRS = HEADS // 2
KEYS = 256
PH = 8
NK = 128
TOPK = 16
SLOTS = PH * TOPK
ROWBUF = 8
EPS = 1e-6

R_ADA1, R_CONV, R_GATE, R_ADAG1, R_PROJ, R_WOUT, R_ADA2, R_PQ, R_ADAG2, ROUNDS = 0, 2, 3, 5, 6, 7, 8, 10, 12, 13

N_RMS1 = 0
N_CONV = 1
N_QKV = N_CONV + 2 * CT
N_GATE = N_QKV + 6
N_LN = N_GATE + 2 * KT
N_PROJ = N_LN + 2
N_WOUT = N_PROJ + 2 * KT
N_RMS2 = N_WOUT + KT
N_TOK = N_RMS2 + 1
N_PQ = N_TOK + 4 * TB
N_G2 = N_PQ + 2 * PH
BANKS = 4


def build(nc, stream, wqkv, skT, xT, cols, rows, biasd, identd, pu, pv, out):
    f32, i32, u32 = mybir.dt.float32, mybir.dt.int32, mybir.dt.uint32
    ALU, ACT, AX = mybir.AluOpType, mybir.ActivationFunctionType, mybir.AxisListType
    NEG = -3.0e38

    with ExitStack() as ctx:
        def sb(name, shape, dt=f32):
            return ctx.enter_context(nc.sbuf_tensor(name, shape, dt))

        def sem(name):
            return ctx.enter_context(nc.semaphore(name))

        wring = sb("wring", [P, 4, 2, KT, P])
        qkvw = sb("qkvw", [P, 6, KT, P])
        hT = sb("hT", [P, KT, T])
        nT = sb("nT", [P, KT, T])
        gates = sb("gates", [P, 2 * KT, T])
        work = sb("work", [P, ROWBUF, D])
        skw = sb("skw", [P, 2 * PH, NK])
        colv = sb("colv", [P, 208])
        rowv = sb("rowv", [P, HEADS + D])
        ident = sb("ident", [P, P])
        ones = sb("ones", [P, P])
        eps = sb("eps", [P, 1])
        cond = sb("cond", [P, KT])
        mod = sb("mod", [P, 6 * KT])
        coef = sb("coef", [P, 2, KT])
        sq = sb("sq", [P, 2, T])
        std = sb("std", [P, T])
        rstd = sb("rstd", [P, T])
        bias = sb("bias", [P, HEADS, KEYS])
        nsink = sb("nsink", [P, HEADS])
        attnT = sb("attnT", [P, PAIRS, T])

        W = work[:, :, :].rearrange("p a b -> p (a b)")
        PADT = T + TAPS - 1
        u = W[:, 0:CT * PADT].rearrange("p (m t) -> p m t", m=CT)
        o0 = CT * PADT
        y = W[:, o0:o0 + CT * T].rearrange("p (m t) -> p m t", m=CT)
        o0 += CT * T
        sg = W[:, o0:o0 + 2 * T].rearrange("p (m t) -> p m t", m=2)
        o0 += 2 * T
        qT = W[:, o0:o0 + PAIRS * T].rearrange("p (m t) -> p m t", m=PAIRS)
        o0 += PAIRS * T
        kT = W[:, o0:o0 + T]
        o0 += T
        vtok = sb("vtok", [P, TB, P])
        ssb = sb("ssb", [P, 2, 2, KEYS])
        pexp = sb("pexp", [P, 2, 2, KEYS])
        ptsb = sb("ptsb", [P, 2, 4, P])
        nmx = sb("nmx", [P, 2, 2])
        mx = sb("mx", [P, 2, 2])
        rs = sb("rs", [P, 2, 2])
        es = sb("es", [P, 2, 2])
        den = sb("den", [P, 2, 2])
        rden = sb("rden", [P, 2, 2])
        assert o0 <= ROWBUF * D

        b_ada, g1, g2 = colv[:, 0:48], colv[:, 48:56], colv[:, 56:64]
        b_dw, ln_g, ln_b = colv[:, 64:68], colv[:, 68:72], colv[:, 72:76]
        w_dw = colv[:, 76:76 + CT * TAPS].rearrange("p (m k) -> p m k", m=CT)
        ccol = colv[:, 200:208]
        gfin = rowv[:, HEADS:HEADS + D]

        Q = qkvw[:, :, :, :].rearrange("p a b c -> p (a b c)")
        qh = Q[:, 0:4 * T].rearrange("p (e s t) -> p e s t", e=2, s=2)
        sc = Q[:, 4 * T:4 * T + 2 * 8 * NK].rearrange("p (e r n) -> p e r n", e=2, r=8)
        o1 = 4 * T + 2 * 8 * NK
        sc2 = Q[:, o1:o1 + 8 * NK].rearrange("p (r n) -> p r n", r=8)
        o1 += 8 * NK
        cand = Q[:, o1:o1 + TB * 256].rearrange("p (b n) -> p b n", b=TB)
        assert o1 + TB * 256 <= 6 * KT * P
        B = bias[:, :, :].rearrange("p a b -> p (a b)")
        cand2 = B[:, 0:TB * 256].rearrange("p (b n) -> p b n", b=TB)
        hot = B[:, TB * 256:2 * TB * 256].rearrange("p (b k a) -> p b k a", b=TB, k=TOPK)
        E = pexp[:, :, :, :].rearrange("p a b c -> p (a b c)")
        four = lambda o: E[:, o:o + TB * 2 * TOPK]
        vals, vidf, vidx = (four(o).rearrange("p (b s k) -> p b s k", b=TB, s=2) for o in (0, 128, 256))
        posa, posf, sel = (four(o).rearrange("p (s b k) -> p s b k", b=TB, s=2) for o in (384, 512, 640))
        best, pos = (E[:, o:o + TB * TOPK].rearrange("p (b k) -> p b k", b=TB) for o in (768, 832))
        vidx, posa, pos = vidx.bitcast(u32), posa.bitcast(u32), pos.bitcast(u32)
        iota16 = sb("iota16", [P, TOPK])
        A4 = attnT[:, :, :].rearrange("p m (a h k) -> p m a h k", h=PH, k=TOPK)
        bests, gw, eidx = A4[:, 0], A4[:, 1], A4[:, 2].bitcast(i32)
        gsum = sb("gsum", [P, TB * PH])
        islot = sb("islot", [P, ROWBUF], i32)
        dot1 = sb("dot1", [P, ROWBUF])
        dots = sb("dots", [P, SLOTS])
        act_w = sb("act_w", [P, SLOTS])
        G = gates[:, :, :].rearrange("p a b -> p (a b)")
        n_tok = G[:, 0:TB * D].rearrange("p (b d) -> p b d", b=TB)
        h_tok = G[:, TB * D:2 * TB * D].rearrange("p (b d) -> p b d", b=TB)
        R2 = wring[:, :, :, :, :].rearrange("p a b c d -> p (a b c d)")
        g2row = R2[:, 0:D]
        acc = R2[:, D:3 * D].rearrange("p (a d) -> p a d", a=2)
        junk = R2[:, 3 * D:4 * D]
        yout = R2[:, 4 * D:6 * D].rearrange("p (a d) -> p a d", a=2)
        ssum = sb("ssum", [P, TB])
        sstd = sb("sstd", [P, TB])
        srstd = sb("srstd", [P, TB])

        ps = ctx.enter_context(nc.psum_tensor("ps", [P, 8, 512], f32))
        PT_B, O_B = ps[:, 6, :], ps[:, 7, :]
        MOD = ps[:, 7, 0:6 * KT]

        small_here = sem("small_here")
        x_here = sem("x_here")
        qkvw_here = sem("qkvw_here")
        late_here = sem("late_here")
        out_done = [sem(f"out_done{e}") for e in range(2)]
        w_here = [sem(f"w_here{s}") for s in range(4)]
        pair_begun = sem("pair_begun")
        consts = sem("consts")
        cond_ready = sem("cond_ready")
        tile_done = sem("tile_done")
        bank_free = [sem(f"bank_free{b}") for b in range(BANKS)]
        mod_done = sem("mod_done")
        mod_ready = sem("mod_ready")
        sq_ready, sq_used = sem("sq_ready"), sem("sq_used")
        scaled = sem("scaled")
        n_ready = sem("n_ready")
        s_done, s_biased = sem("s_done"), sem("s_biased")
        nmx_ready, exp_done, p_ready = sem("nmx_ready"), sem("exp_done"), sem("p_ready")
        pt_done, pt_ready = sem("pt_done"), sem("pt_ready")
        o_done, o_ready = sem("o_done"), sem("o_ready")
        dve_step = sem("dve_step")
        dve_turn = sem("dve_turn")
        y_ready, yc_ready, yn_ready, silu_ready = sem("y_ready"), sem("yc_ready"), sem("yn_ready"), sem("silu_ready")
        merged = sem("merged")
        sc_done, sc_ready, sc_free = sem("sc_done"), sem("sc_ready"), sem("sc_free")
        sm_in, sm_exp = sem("sm_in"), sem("sm_exp")
        idx_ready = sem("idx_ready")
        g_ready = sem("g_ready")
        slot_copied, pool_turn = sem("slot_copied"), sem("pool_turn")
        row_here = [sem(f"row_here{b}") for b in range(ROWBUF)]
        row_used = sem("row_used")
        dots_ready, gelu_ready = sem("dots_ready"), sem("gelu_ready")
        y_sum, y_sq, y_std, y_out = sem("y_sum"), sem("y_sq"), sem("y_std"), sem("y_out")

        def freed(eng, n):
            eng.wait_ge(bank_free[n % BANKS], n // BANKS + 1)

        block = ctx.enter_context(nc.Block())

        @block.sync
        def _(sp):
            sp.dma_start(colv[:, :], cols).then_inc(small_here, 16)
            sp.dma_start(hT[:, :, :], xT).then_inc(x_here, 16)

            def load_round(r, wait):
                for s in range(4):
                    if wait:
                        sp.wait_ge(pair_begun, r * 4 + s - 2)
                    sp.dma_start(wring[:, s, :, :, :].rearrange("p a b c -> p (a b c)"),
                                 stream[bass.ds(r * 4 + s, 1), :, :].rearrange("a p f -> (a p) f")
                                 ).then_inc(w_here[s], 16)
            load_round(0, False)
            sp.dma_start(ident[:, :], identd).then_inc(late_here, 16)
            sp.dma_start(rowv[:, :], rows).then_inc(late_here, 16)
            sp.dma_start(bias[:, :, :], biasd).then_inc(late_here, 16)
            sp.dma_start(skw[:, :, :], skT).then_inc(late_here, 16)
            sp.dma_start(qkvw[:, :, :, :], wqkv).then_inc(qkvw_here, 16)
            with sp.Fori(1, ROUNDS) as r:
                load_round(r, True)
            for b in range(TB):
                sp.wait_ge(y_out, b + 1)
                sp.dma_start(out[b * P:(b + 1) * P, :], yout[:, b % 2, :]).then_inc(out_done[b % 2], 16)
            for e in range(2):
                sp.wait_ge(out_done[e], 16 * TB // 2)

        @block.gpsimd
        def _(pool):
            nc.gpsimd.memset(ones[:, :], 1.0).then_inc(consts, 1)
            nc.gpsimd.memset(eps[:, :], EPS).then_inc(consts, 1)
            nc.gpsimd.memset(u[:, :, 0:TAPS - 1], 0.0).then_inc(consts, 1)
            nc.gpsimd.iota(iota16[:, :], pattern=[[1, TOPK]], base=0, channel_multiplier=0,
                           allow_small_or_imprecise_dtypes=True).then_inc(consts, 1)

            n = 0
            pool.wait_ge(idx_ready, PH)
            for b in range(TB):
                for table in (pu, pv):
                    def fetch(k0, wait):
                        for s in range(ROWBUF):
                            if wait:
                                pool.wait_ge(row_used, k0 + n - ROWBUF + s + 1)
                            nc.gpsimd.tensor_copy(islot[:, s:s + 1],
                                                  eidx[:, b, :, :].rearrange("p h k -> p (h k)")[:, bass.ds(k0 + s, 1)]
                                                  ).then_inc(slot_copied, 1)
                            pool.wait_ge(slot_copied, k0 + n + s + 1)
                            nc.gpsimd.sem_inc(pool_turn, 1)
                            nc.gpsimd.indirect_dma_start(
                                out=work[:, s, :], out_offset=None, in_=table,
                                in_offset=bass.IndirectOffsetOnAxis(ap=islot[:, s:s + 1], axis=0)
                            ).then_inc(row_here[s], 16)
                    if n == 0:
                        fetch(0, False)
                    with pool.Fori(1 if n == 0 else 0, SLOTS // ROWBUF) as group:
                        fetch(group * ROWBUF, True)
                    n += SLOTS

        @block.tensor
        def _(pe):
            def bank(n):
                if n >= BANKS:
                    pe.wait_ge(bank_free[n % BANKS], n // BANKS)
                return ps[:, n % BANKS, :]

            def column_sums(n, sq0, count):
                o = bank(n)
                for k in range(count):
                    pe.wait_ge(sq_ready, sq0 + k + 1)
                    mm = nc.tensor.matmul(o, ones[:, :], sq[:, (sq0 + k) % 2, :], start=(k == 0), stop=(k == count - 1))
                    mm.then_inc(sq_used if k < count - 1 else tile_done, 1)

            def ada(r, tile0):
                for s in range(4):
                    pe.wait_ge(w_here[s], (r + 1) * 16)
                    for j in range(2):
                        for k in range(KT):
                            mm = nc.tensor.matmul(MOD[:, tile0 + 2 * s + j:tile0 + 2 * s + j + 1],
                                                  wring[:, s, j, k, :], cond[:, k:k + 1],
                                                  start=(k == 0), stop=(k == KT - 1))
                            if j + k == 0:
                                mm.then_inc(pair_begun, 1)
                return mm

            def product(o, lhs, rhs, count=KT, begins=False):
                for k in range(count):
                    mm = nc.tensor.matmul(o, lhs(k), rhs(k), start=(k == 0), stop=(k == count - 1))
                    if begins and k == 0:
                        mm.then_inc(pair_begun, 1)
                return mm

            pe.wait_ge(consts, 1)
            column_sums(N_RMS1, 0, KT)
            pe.wait_ge(cond_ready, 1)
            ada(0, 0)
            ada(1, KT).then_inc(mod_done, 1)

            pe.wait_ge(n_ready, KT)
            for s in range(4):
                pe.wait_ge(w_here[s], (R_CONV + 1) * 16)
                for j in range(2):
                    mm = product(bank(N_CONV + 2 * s + j), lambda k: wring[:, s, j, k, :], lambda k: nT[:, k, :], begins=j == 0)
                    mm.then_inc(tile_done, 1)

            pe.wait_ge(qkvw_here, 16)
            for j in range(5):
                mm = product(bank(N_QKV + j), lambda k: qkvw[:, j, k, :], lambda k: nT[:, k, :])
                mm.then_inc(tile_done, 1)
            o = bank(N_QKV + 5)
            for b in range(TB):
                mm = product(o[:, b * P:(b + 1) * P], lambda k: nT[:, k, b * P:(b + 1) * P], lambda k: qkvw[:, 5, k, :])
            mm.then_inc(tile_done, 1)

            for j in range(2, 6):
                freed(pe, N_QKV + j)
            pe.wait_ge(late_here, 64)

            def att_scores(a):
                b, m = divmod(a, PAIRS)
                if a >= 2:
                    pe.wait_ge(s_biased, a - 1)
                k0, c0 = (0, P) if b == 0 else ((b - 1) * P, 0)
                for e in range(2):
                    mm = nc.tensor.matmul(ps[:, 2 * (a % 2) + e, c0:KEYS], qT[e * HD:(e + 1) * HD, m, b * P:(b + 1) * P],
                                          kT[e * HD:(e + 1) * HD, k0:(b + 1) * P], start=True, stop=True)
                mm.then_inc(s_done, 1)

            def att_out(a):
                b, m = divmod(a, PAIRS)
                tiles = (1,) if b == 0 else (0, 1)
                pe.wait_ge(p_ready, a + 1)
                if a >= 1:
                    pe.wait_ge(pt_ready, a)
                for e in range(2):
                    for c in tiles:
                        mm = nc.tensor.transpose(PT_B[:, (2 * e + c) * P:(2 * e + c + 1) * P],
                                                 pexp[:, a % 2, e, c * P:(c + 1) * P], ident[:, :])
                mm.then_inc(pt_done, 1)
                if a + 2 < TB * PAIRS:
                    att_scores(a + 2)
                pe.wait_ge(pt_ready, a + 1)
                if m == 0 and b >= 1:
                    pe.wait_ge(o_ready, b)
                for e in range(2):
                    for c in tiles:
                        mm = nc.tensor.matmul(O_B[e * HD:(e + 1) * HD, m * P:(m + 1) * P],
                                              vtok[:, b - 1 + c, e * HD:(e + 1) * HD], ptsb[:, a % 2, 2 * e + c, :],
                                              start=(c == tiles[0]), stop=(c == 1))
                if m == PAIRS - 1:
                    mm.then_inc(o_done, 1)

            att_scores(0)
            att_scores(1)
            for a in range(TB * PAIRS):
                att_out(a)

            pe.wait_ge(s_biased, TB * PAIRS)
            with pe.Fori(0, 2) as r:
                for s in range(4):
                    pe.wait_ge(w_here[s], (r + R_GATE + 1) * 16)
                    for j in range(2):
                        n0 = N_GATE + 2 * s + j
                        pe.wait_ge(bank_free[n0 % BANKS], r * 2 + n0 // BANKS)
                        mm = product(ps[:, n0 % BANKS, :], lambda k: wring[:, s, j, k, :], lambda k: nT[:, k, :], begins=j == 0)
                        mm.then_inc(tile_done, 1)

            pe.wait_ge(o_ready, TB)
            ada(R_ADAG1, 2 * KT).then_inc(mod_done, 1)

            o = bank(N_LN)
            pe.wait_ge(y_ready, CT)
            mm = product(o, lambda k: ones[:, :], lambda k: y[:, k, :], CT)
            mm.then_inc(tile_done, 1)
            column_sums(N_LN + 1, KT, CT)

            pe.wait_ge(silu_ready, CT)
            for s in range(4):
                pe.wait_ge(w_here[s], (R_PROJ + 1) * 16)
                for j in range(2):
                    n = N_PROJ + 4 * s + 2 * j
                    mm = product(bank(n), lambda k: wring[:, s, j, k, :], lambda k: y[:, k, :], CT, begins=j == 0)
                    mm.then_inc(tile_done, 1)
                    mm = product(bank(n + 1), lambda k: wring[:, s, j, CT + k, :], lambda k: attnT[:, k, :], CT)
                    mm.then_inc(tile_done, 1)

            pe.wait_ge(merged, KT)
            for s in range(4):
                pe.wait_ge(w_here[s], (R_WOUT + 1) * 16)
                for j in range(2):
                    mm = product(bank(N_WOUT + 2 * s + j), lambda k: wring[:, s, j, k, :], lambda k: gates[:, k, :],
                                 begins=j == 0)
                    mm.then_inc(tile_done, 1)

            column_sums(N_RMS2, KT + CT, KT)
            pe.wait_ge(mod_ready, 2)
            ada(R_ADA2, 3 * KT)
            ada(R_ADA2 + 1, 4 * KT).then_inc(mod_done, 1)

            pe.wait_ge(n_ready, 2 * KT)
            for w, src in enumerate((nT, hT)):
                for b in range(TB):
                    for half in range(2):
                        o = bank(N_TOK + 2 * TB * w + 2 * b + half)
                        for q in range(4):
                            mm = nc.tensor.transpose(o[:, q * P:(q + 1) * P],
                                                     src[:, 4 * half + q, b * P:(b + 1) * P], ident[:, :])
                        mm.then_inc(tile_done, 1)

            with pe.Fori(0, 2) as r:
                for s in range(4):
                    pe.wait_ge(w_here[s], (r + R_PQ + 1) * 16)
                    for j in range(2):
                        n0 = N_PQ + 2 * s + j
                        pe.wait_ge(bank_free[n0 % BANKS], r * 2 + n0 // BANKS)
                        mm = product(ps[:, n0 % BANKS, :], lambda k: wring[:, s, j, k, :], lambda k: nT[:, k, :], begins=j == 0)
                        mm.then_inc(tile_done, 1)
                    pe.wait_ge(bank_free[(N_PQ + 2 * s) % BANKS], r * 2 + (N_PQ + 2 * s) // BANKS + 1)
                    pe.wait_ge(bank_free[(N_PQ + 2 * s + 1) % BANKS], r * 2 + (N_PQ + 2 * s + 1) // BANKS + 1)
                    pe.wait_ge(sc_ready, r * 4 + s + 1)
                    for b in range(TB):
                        for half in range(2):
                            mm = nc.tensor.matmul(
                                ps[:, 4 + b // 2, ((b % 2) * 2 + half) * NK:((b % 2) * 2 + half + 1) * NK],
                                qh[:, s % 2, half, b * P:(b + 1) * P],
                                skw[:, bass.ds(r * 8 + 2 * s + half, 1), :].rearrange("p a n -> p (a n)"),
                                start=True, stop=True)
                    mm.then_inc(sc_done, 1)

            pe.wait_ge(mod_ready, 3)
            ada(R_ADAG2, 5 * KT).then_inc(mod_done, 1)
            pe.wait_ge(mod_ready, 5)
            for half in range(2):
                o = bank(N_G2 + half)
                for q in range(4):
                    mm = nc.tensor.matmul(o[:, q * P:(q + 1) * P], ones[:, :],
                                          hT[:, 4 * half + q, 0:P], start=True, stop=True)
                mm.then_inc(tile_done, 1)

        @block.scalar
        def _(act):
            f = nc.scalar.activation
            act.wait_ge(small_here, 16)
            f(cond[:, :], ccol, ACT.Silu).then_inc(cond_ready, 1)

            def squares(src, n0, used, count, need):
                for k in range(count):
                    need(k)
                    if k >= 2:
                        act.wait_ge(sq_used, used + k - 1)
                    f(sq[:, (n0 + k) % 2, :], src(k), ACT.Square).then_inc(sq_ready, 1)

            def root(n, count):
                act.wait_ge(tile_done, n + 1)
                f(std[:, :], ps[:, n % BANKS, :], ACT.Sqrt, bias=eps[:, 0:1], scale=1.0 / count
                  ).then_inc(bank_free[n % BANKS], 1)

            def modulate(stage, shift0):
                for k in range(KT):
                    act.wait_ge(scaled, stage * KT + k + 1)
                    f(nT[:, k, :], nT[:, k, :], ACT.Identity, scale=coef[:, stage, k:k + 1],
                      bias=mod[:, shift0 + k:shift0 + k + 1]).then_inc(n_ready, 1)

            act.wait_ge(x_here, 16)
            squares(lambda k: hT[:, k, :], 0, 0, KT, lambda k: None)
            act.wait_ge(consts, 3)
            root(N_RMS1, D)
            act.wait_ge(mod_ready, 1)
            modulate(0, 0)

            for m in range(CT):
                n = N_CONV + 2 * m + 1
                act.wait_ge(tile_done, n + 1)
                if m >= 2:
                    freed(act, n - 5)
                f(sg[:, m % 2, :], ps[:, n % BANKS, :], ACT.Sigmoid).then_inc(bank_free[n % BANKS], 1)
            for j in range(6):
                n = N_QKV + j
                act.wait_ge(tile_done, n + 1)
                dst = (qT[:, j, :] if j < 4 else kT[:, :] if j == 4 else
                       vtok[:, :, :].rearrange("p b d -> p (b d)"))
                f(dst, ps[:, n % BANKS, :], ACT.Copy, scale=HD ** -0.5 if j < 4 else 1.0
                  ).then_inc(bank_free[n % BANKS], 1)

            def att_evac(a):
                b = a // PAIRS
                act.wait_ge(pt_done, a + 1)
                s0 = P if b == 0 else 0
                view = lambda t: t.rearrange("p (e k) -> p e k", e=2)[:, :, s0:KEYS]
                f(view(ptsb[:, a % 2, :, :].rearrange("p c q -> p (c q)")), view(PT_B), ACT.Copy).then_inc(pt_ready, 1)
                if a % PAIRS == PAIRS - 1:
                    act.wait_ge(o_done, b + 1)
                    f(attnT[:, :, b * P:(b + 1) * P], O_B.rearrange("p (m q) -> p m q", m=PAIRS), ACT.Copy
                      ).then_inc(o_ready, 1)
            for a in range(TB * PAIRS):
                c0 = P if a < PAIRS else 0
                act.wait_ge(nmx_ready, a + 1)
                if a >= 2:
                    act.wait_ge(pt_done, a - 1)
                for e in range(2):
                    f(pexp[:, a % 2, e, c0:KEYS], ssb[:, a % 2, e, c0:KEYS], ACT.Exp, bias=nmx[:, a % 2, e:e + 1],
                      accum_out=rs[:, a % 2, e:e + 1])
                f(es[:, a % 2, :], mx[:, a % 2, :], ACT.Exp).then_inc(exp_done, 1)
                if a >= 1:
                    att_evac(a - 1)
            att_evac(TB * PAIRS - 1)

            with act.Fori(0, 2 * KT // 4) as t4:
                t = t4 * 4
                for j in range(4):
                    act.wait_ge(tile_done, t + N_GATE + j + 1)
                    f(gates[:, bass.ds(t + j, 1), :].rearrange("p a t -> p (a t)"),
                      ps[:, (N_GATE + j) % BANKS, :], ACT.Sigmoid).then_inc(bank_free[(N_GATE + j) % BANKS], 1)

            squares(lambda k: y[:, k, :], KT, KT - 1, CT, lambda k: act.wait_ge(yc_ready, k + 1))
            root(N_LN + 1, CT * P)
            for m in range(CT):
                act.wait_ge(yn_ready, m + 1)
                f(y[:, m, :], y[:, m, :], ACT.Silu, scale=ln_g[:, m:m + 1], bias=ln_b[:, m:m + 1]).then_inc(silu_ready, 1)

            squares(lambda k: hT[:, k, :], KT + CT, KT + CT - 2, KT, lambda k: freed(act, N_WOUT + k))
            root(N_RMS2, D)
            act.wait_ge(mod_ready, 3)
            modulate(1, 3 * KT)

            for w, dst in enumerate((n_tok, h_tok)):
                for b in range(TB):
                    for half in range(2):
                        n = N_TOK + 2 * TB * w + 2 * b + half
                        act.wait_ge(tile_done, n + 1)
                        f(dst[:, b, half * T:(half + 1) * T], ps[:, n % BANKS, :], ACT.Copy
                          ).then_inc(bank_free[n % BANKS], 1)

            nc.scalar.sem_inc(sc_ready, 1)
            nc.scalar.sem_inc(sc_free, 2)
            with act.Fori(0, PH // 2) as h2:
                h = h2 * 2
                for e in range(2):
                    for half in range(2):
                        n0 = N_PQ + 2 * e + half
                        act.wait_ge(tile_done, h * 2 + n0 + 1)
                        f(qh[:, e, half, :], ps[:, n0 % BANKS, :], ACT.Copy).then_inc(bank_free[n0 % BANKS], 1)
                    act.wait_ge(sc_done, h + e + 1)
                    act.wait_ge(sc_free, h + e + 1)
                    for c in range(2):
                        i = f(sc[:, e, 4 * c:4 * c + 4, :].rearrange("p r n -> p (r n)"), ps[:, 4 + c, :], ACT.Copy)
                    i.then_inc(sc_ready, 1)

            act.wait_ge(sm_in, 1)
            f(gw[:, :, :, :], gw[:, :, :, :], ACT.Exp).then_inc(sm_exp, 1)
            for half in range(2):
                n = N_G2 + half
                act.wait_ge(tile_done, n + 1)
                f(g2row[:, half * T:(half + 1) * T], ps[:, n % BANKS, :], ACT.Copy).then_inc(bank_free[n % BANKS], 1)
            for b in range(TB):
                act.wait_ge(dots_ready, (b + 1) * (SLOTS // ROWBUF))
                f(act_w[:, :], dots[:, :], ACT.Gelu).then_inc(gelu_ready, 1)
                act.wait_ge(y_sum, b + 1)
                f(junk, yout[:, b % 2, :], ACT.Square, accum_out=ssum[:, b:b + 1]).then_inc(y_sq, 1)
                act.wait_ge(y_sq, b + 1)
                f(sstd[:, b:b + 1], ssum[:, b:b + 1], ACT.Sqrt, bias=eps[:, 0:1], scale=1.0 / D).then_inc(y_std, 1)

        @block.vector
        def _(dve):
            v = nc.vector
            count = [0]

            def step(ins):
                count[0] += 1
                ins.then_inc(dve_step, 1)

            def settled():
                dve.wait_ge(dve_step, count[0])

            def scale_rows(stage):
                n = N_RMS2 if stage else N_RMS1
                freed(dve, n)
                step(v.reciprocal(rstd[:, :], std[:, :]))
                settled()
                for k in range(KT):
                    if stage and k == 0:
                        dve.wait_ge(tile_done, N_GATE + 2 * KT)
                    v.tensor_tensor(nT[:, k, :], hT[:, k, :], rstd[:, :], ALU.mult).then_inc(scaled, 1)

            def take_mod(done, c0, c1):
                dve.wait_ge(mod_done, done)
                return v.tensor_tensor(mod[:, c0:c1], MOD[:, c0:c1], b_ada[:, c0:c1], ALU.add)

            dve.wait_ge(x_here, 16)
            scale_rows(0)
            dve.wait_ge(small_here, 16)
            step(take_mod(1, 0, 2 * KT))
            settled()
            v.scalar_tensor_tensor(coef[:, 0, :], mod[:, KT:2 * KT], 1.0, g1, ALU.add, ALU.mult).then_inc(mod_ready, 1)

            dve.wait_ge(consts, 4)
            for m in range(CT):
                n = N_CONV + 2 * m
                dve.wait_ge(tile_done, n + 1)
                freed(dve, n + 1)
                v.tensor_tensor(u[:, m, TAPS - 1:PADT], ps[:, n % BANKS, :], sg[:, m % 2, :], ALU.mult
                                ).then_inc(bank_free[n % BANKS], 1)

            dve.wait_ge(late_here, 64)
            step(v.tensor_scalar(nsink[:, :], rowv[:, 0:HEADS], -1.0, None, ALU.mult))
            settled()

            def att_norm(a):
                c0 = P if a < PAIRS else 0
                dve.wait_ge(exp_done, a + 1)
                step(v.tensor_tensor(den[:, a % 2, :], rs[:, a % 2, :], es[:, a % 2, :], ALU.add))
                settled()
                step(v.reciprocal(rden[:, a % 2, :], den[:, a % 2, :]))
                settled()
                for e in range(2):
                    i = v.tensor_scalar(pexp[:, a % 2, e, c0:KEYS], pexp[:, a % 2, e, c0:KEYS],
                                        rden[:, a % 2, e:e + 1], None, ALU.mult)
                i.then_inc(p_ready, 1)

            for a in range(TB * PAIRS):
                m = a % PAIRS
                c0 = P if a < PAIRS else 0
                S = ps[:, 2 * (a % 2):2 * (a % 2) + 2, :]
                dve.wait_ge(s_done, a + 1)
                if a >= 2:
                    dve.wait_ge(exp_done, a - 1)
                v.tensor_tensor(ssb[:, a % 2, :, c0:KEYS], S[:, :, c0:KEYS], bias[:, 2 * m:2 * m + 2, c0:KEYS],
                                ALU.add).then_inc(s_biased, 1)
                dve.wait_ge(s_biased, a + 1)
                step(v.tensor_reduce(mx[:, a % 2, :], ssb[:, a % 2, :, c0:KEYS], axis=AX.X, op=ALU.max))
                settled()
                step(v.scalar_tensor_tensor(nmx[:, a % 2, :], mx[:, a % 2, :], -1.0, nsink[:, 2 * m:2 * m + 2],
                                            ALU.mult, ALU.min))
                settled()
                v.tensor_tensor(mx[:, a % 2, :], nmx[:, a % 2, :], nsink[:, 2 * m:2 * m + 2], ALU.subtract
                                ).then_inc(nmx_ready, 1)
                if a >= 1:
                    att_norm(a - 1)
            att_norm(TB * PAIRS - 1)

            for k in range(TAPS):
                base = count[0]
                for m in range(CT):
                    if k == 0:
                        i = v.tensor_scalar(y[:, m, :], u[:, m, 0:T], w_dw[:, m, 0:1], b_dw[:, m:m + 1],
                                            ALU.mult, ALU.add)
                    else:
                        dve.wait_ge(dve_step, base - CT + m + 1)
                        i = v.scalar_tensor_tensor(y[:, m, :], u[:, m, k:k + T], w_dw[:, m, k:k + 1], y[:, m, :],
                                                   ALU.mult, ALU.add)
                    if k < TAPS - 1:
                        step(i)
                    else:
                        i.then_inc(y_ready, 1)
            take_mod(2, 2 * KT, 3 * KT).then_inc(mod_ready, 1)

            dve.wait_ge(y_ready, CT)
            dve.wait_ge(tile_done, N_LN + 1)
            v.tensor_scalar(rstd[:, :], ps[:, N_LN % BANKS, :], 1.0 / (CT * P), None, ALU.mult
                            ).then_inc(bank_free[N_LN % BANKS], 1)
            freed(dve, N_LN)
            for m in range(CT):
                v.tensor_tensor(y[:, m, :], y[:, m, :], rstd[:, :], ALU.subtract).then_inc(yc_ready, 1)
            freed(dve, N_LN + 1)
            step(v.reciprocal(rstd[:, :], std[:, :]))
            settled()
            dve.wait_ge(yc_ready, CT)
            for m in range(CT):
                v.tensor_tensor(y[:, m, :], y[:, m, :], rstd[:, :], ALU.mult).then_inc(yn_ready, 1)

            for d in range(KT):
                n = N_PROJ + 2 * d
                if d == 0:
                    for q in range(4):
                        freed(dve, N_GATE + 2 * KT - 4 + q)
                dve.wait_ge(tile_done, n + 2)
                v.tensor_tensor(gates[:, d, :], ps[:, n % BANKS, :], gates[:, d, :], ALU.mult
                                ).then_inc(bank_free[n % BANKS], 1)
                v.tensor_tensor(gates[:, KT + d, :], ps[:, (n + 1) % BANKS, :], gates[:, KT + d, :], ALU.mult
                                ).then_inc(bank_free[(n + 1) % BANKS], 1)
                freed(dve, n)
                freed(dve, n + 1)
                v.tensor_tensor(gates[:, d, :], gates[:, d, :], gates[:, KT + d, :], ALU.add).then_inc(merged, 1)

            dve.wait_ge(mod_ready, 2)
            for d in range(KT):
                n = N_WOUT + d
                dve.wait_ge(tile_done, n + 1)
                v.scalar_tensor_tensor(hT[:, d, :], ps[:, n % BANKS, :], mod[:, 2 * KT + d:2 * KT + d + 1], hT[:, d, :],
                                       ALU.mult, ALU.add).then_inc(bank_free[n % BANKS], 1)
            for k in range(4, KT):
                freed(dve, N_WOUT + k)
            scale_rows(1)
            step(take_mod(3, 3 * KT, 5 * KT))
            settled()
            v.scalar_tensor_tensor(coef[:, 1, :], mod[:, 4 * KT:5 * KT], 1.0, g2, ALU.add, ALU.mult
                                   ).then_inc(mod_ready, 1)

            base = count[0]
            per = [0]

            def hstep(ins, h):
                per[0] += 1
                ins.then_inc(dve_step, 1)

            def hsettled(h, e, k):
                dve.wait_ge(dve_step, h * k + base + per[0])
                v.sem_inc(dve_turn, 1)

            STEPS = 74
            with dve.Fori(0, PH // 2) as h2:
                h = h2 * 2
                per[0] = 0
                for e in range(2):
                    start = per[0]
                    dve.wait_ge(sc_ready, h + e + 2)
                    v.sem_inc(dve_turn, 1)
                    for b in range(TB):
                        for half in range(2):
                            hstep(v.max(vals[:, b, half, 0:8], sc[:, e, 2 * b + half, :]), h)
                    hsettled(h, e, STEPS)
                    for b in range(TB):
                        for half in range(2):
                            hstep(v.match_replace(out=sc2[:, 2 * b + half, :], in_to_replace=vals[:, b, half, 0:8],
                                                  in_values=sc[:, e, 2 * b + half, :], imm_value=NEG), h)
                            hstep(v.max_index(out=vidx[:, b, half, 0:8], in_max=vals[:, b, half, 0:8],
                                              in_values=sc[:, e, 2 * b + half, :]), h)
                    hsettled(h, e, STEPS)
                    for b in range(TB):
                        for half in range(2):
                            hstep(v.max(vals[:, b, half, 8:16], sc2[:, 2 * b + half, :]), h)
                    hsettled(h, e, STEPS)
                    for b in range(TB):
                        for half in range(2):
                            i = v.max_index(out=vidx[:, b, half, 8:16], in_max=vals[:, b, half, 8:16],
                                            in_values=sc2[:, 2 * b + half, :])
                            hstep(i, h)
                    for b in range(TB):
                        hstep(v.tensor_tensor(cand[:, b, :].rearrange("p (i j) -> p i j", i=TOPK),
                                              vals[:, b, 0, :].unsqueeze(2).broadcast_to([P, TOPK, TOPK]),
                                              vals[:, b, 1, :].unsqueeze(1).broadcast_to([P, TOPK, TOPK]), ALU.add), h)
                    hsettled(h, e, STEPS)
                    v.tensor_copy(vidf[:, :, :, :], vidx[:, :, :, :]).then_inc(sc_free, 1)
                    for b in range(TB):
                        hstep(v.max(best[:, b, 0:8], cand[:, b, :]), h)
                    hsettled(h, e, STEPS)
                    for b in range(TB):
                        hstep(v.match_replace(out=cand2[:, b, :], in_to_replace=best[:, b, 0:8],
                                              in_values=cand[:, b, :], imm_value=NEG), h)
                        hstep(v.max_index(out=pos[:, b, 0:8], in_max=best[:, b, 0:8], in_values=cand[:, b, :]), h)
                    hsettled(h, e, STEPS)
                    for b in range(TB):
                        hstep(v.max(best[:, b, 8:16], cand2[:, b, :]), h)
                    hsettled(h, e, STEPS)
                    for b in range(TB):
                        hstep(v.max_index(out=pos[:, b, 8:16], in_max=best[:, b, 8:16], in_values=cand2[:, b, :]), h)
                    hstep(v.tensor_copy(bests[:, :, bass.ds(h + e, 1), :].rearrange("p b a k -> p b (a k)"),
                                        best[:, :, :]), h)
                    hsettled(h, e, STEPS)
                    hstep(v.tensor_scalar(posa[:, 0, :, :], pos[:, :, :], 4, None, ALU.logical_shift_right), h)
                    hstep(v.tensor_scalar(posa[:, 1, :, :], pos[:, :, :], 15, None, ALU.bitwise_and), h)
                    hsettled(h, e, STEPS)
                    hstep(v.tensor_copy(posf[:, :, :, :], posa[:, :, :, :]), h)
                    hsettled(h, e, STEPS)
                    hotv = hot.rearrange("p b k a -> p (b k) a")
                    for half in range(2):
                        hstep(v.tensor_tensor(hotv, posf[:, half, :, :].rearrange("p b k -> p (b k)").unsqueeze(2)
                                              .broadcast_to([P, TB * TOPK, TOPK]),
                                              iota16[:, :].unsqueeze(1).broadcast_to([P, TB * TOPK, TOPK]),
                                              ALU.is_equal), h)
                        hsettled(h, e, STEPS)
                        if half == 0:
                            dve.wait_ge(sc_free, h + e + 3)
                        hstep(v.tensor_tensor(hot, hot, vidf[:, :, half, :].unsqueeze(2)
                                              .broadcast_to([P, TB, TOPK, TOPK]), ALU.mult), h)
                        hsettled(h, e, STEPS)
                        hstep(v.tensor_reduce(sel[:, half, :, :], hot, axis=AX.X, op=ALU.add), h)
                        hsettled(h, e, STEPS)
                    v.scalar_tensor_tensor(eidx[:, :, bass.ds(h + e, 1), :].rearrange("p b a k -> p b (a k)"),
                                           sel[:, 0, :, :], float(NK), sel[:, 1, :, :], ALU.mult, ALU.add
                                           ).then_inc(idx_ready, 1)
                    dve.wait_ge(idx_ready, h + e + 1)
                assert per[0] == 2 * STEPS, per
            count[0] = base + PH * STEPS

            v.tensor_tensor(gw[:, :, :, :], bests[:, :, :, :], bests[:, :, :, 0:1].broadcast_to([P, TB, PH, TOPK]),
                            ALU.subtract).then_inc(sm_in, 1)
            dve.wait_ge(sm_exp, 1)
            step(v.tensor_reduce(gsum[:, :], gw[:, :, :, :].rearrange("p b h k -> p (b h) k"), axis=AX.X, op=ALU.add))
            settled()
            step(v.reciprocal(gsum[:, :], gsum[:, :]))
            settled()
            gv = gw[:, :, :, :].rearrange("p b h k -> p (b h) k")
            step(v.tensor_tensor(gv, gv, gsum[:, :].unsqueeze(2).broadcast_to([P, TB * PH, TOPK]), ALU.mult))
            take_mod(4, 5 * KT, 6 * KT).then_inc(mod_ready, 1)
            dve.wait_ge(mod_ready, 4)
            freed(dve, N_TOK + 4 * TB - 1)
            for k in range(KT):
                i = v.tensor_scalar(hT[:, k, 0:P], ident[:, :], mod[:, 5 * KT + k:5 * KT + k + 1], None, ALU.mult)
            i.then_inc(mod_ready, 1)

            n = 0
            for b in range(TB):
                with dve.Fori(0, SLOTS // ROWBUF) as group:
                    k0 = group * ROWBUF
                    for s in range(ROWBUF):
                        dve.wait_ge(row_here[s], k0 * 2 + 16 * (n // ROWBUF + 1))
                        v.tensor_tensor_reduce(out=work[:, s, :], in0=work[:, s, :], in1=n_tok[:, b, :], scale=1.0, scalar=0.0,
                                               op0=ALU.mult, op1=ALU.add, accum_out=dot1[:, s:s + 1]
                                               ).then_inc(row_used, 1)
                    dve.wait_ge(row_used, k0 + n + ROWBUF)
                    v.tensor_copy(dots[:, bass.ds(k0, ROWBUF)], dot1[:, :]).then_inc(dots_ready, 1)
                    dve.wait_ge(dots_ready, group + (b * (SLOTS // ROWBUF) + 1))
                n += SLOTS
                dve.wait_ge(gelu_ready, b + 1)
                step(v.tensor_tensor(act_w[:, :], act_w[:, :], gw[:, b, :, :].rearrange("p h k -> p (h k)"), ALU.mult))
                for a in range(2):
                    step(v.memset(acc[:, a, :], 0.0))
                settled()
                with dve.Fori(0, SLOTS // ROWBUF) as group:
                    k0 = group * ROWBUF
                    for s in range(ROWBUF):
                        dve.wait_ge(row_here[s], k0 * 2 + 16 * (n // ROWBUF + 1))
                        dve.wait_ge(row_used, k0 + (n + s - 1))
                        v.scalar_tensor_tensor(acc[:, s % 2, :], work[:, s, :], act_w[:, bass.ds(k0 + s, 1)],
                                               acc[:, s % 2, :], ALU.mult, ALU.add).then_inc(row_used, 1)
                n += SLOTS
                dve.wait_ge(row_used, n)
                step(v.tensor_tensor(acc[:, 0, :], acc[:, 0, :], acc[:, 1, :], ALU.add))
                settled()
                if b == 0:
                    freed(dve, N_G2)
                    freed(dve, N_G2 + 1)
                    for q in range(4):
                        freed(dve, N_TOK + 4 * TB - 4 + q)
                step(v.tensor_tensor(acc[:, 0, :], acc[:, 0, :], g2row, ALU.mult))
                settled()
                if b >= 2:
                    dve.wait_ge(out_done[b % 2], 16 * (b // 2))
                v.tensor_tensor(yout[:, b % 2, :], acc[:, 0, :], h_tok[:, b, :], ALU.add).then_inc(y_sum, 1)
                dve.wait_ge(y_std, b + 1)
                step(v.reciprocal(srstd[:, b:b + 1], sstd[:, b:b + 1]))
                settled()
                v.scalar_tensor_tensor(yout[:, b % 2, :], yout[:, b % 2, :], srstd[:, b:b + 1], gfin, ALU.mult, ALU.mult
                                       ).then_inc(y_out, 1)


def slope_bias():
    slopes = (2.0 ** (-8.0 * np.arange(1, HEADS + 1) / HEADS)).astype(np.float32)
    q = np.arange(P)[:, None] + P
    k = np.arange(KEYS)[None, :]
    chunk = k // HD - q // HD
    seen = (chunk == 0) | (chunk == -1)
    dist = np.abs(q - k).astype(np.float32)
    order = [m + PAIRS * e for m in range(PAIRS) for e in range(2)]
    return np.stack([np.where(seen, -slopes[h] * dist, np.float32(-1e30)) for h in order], 1).astype(np.float32)


def tiles(w):
    n = w.shape[1] // P
    return w.reshape(-1, P, n, P).transpose(2, 1, 0, 3).reshape(n, P, -1)


def kernel(x, c, w_ada, b_ada, g_norm1, w_in, w_dw, b_dw, ln_g, ln_b, w_conv_out, w_attn_out, attn_sinks, w_out,
           g_norm2, w_pq, sub_keys, peer_u, peer_v, g_final):
    import concourse.bacc as _bacc
    from concourse import mybir as _mybir
    from concourse.bass_utils import run_bass_kernel_spmd as _run

    A = np.asarray
    w_in = A(w_in)[0]
    pair = [m + PAIRS * e for m in range(PAIRS) for e in range(2)]
    w_q = w_in[:, 1024:1536].reshape(D, HEADS, HD)[:, pair].reshape(D, -1)
    w_ao = A(w_attn_out)[0].reshape(HEADS, HD, D)[pair].reshape(-1, D)
    conv = tiles(w_in[:, 0:1024])[[0, 4, 1, 5, 2, 6, 3, 7]]
    ada = tiles(A(w_ada)[0])
    stream = np.concatenate([ada[0:16], conv, tiles(w_in[:, 1792:3840]), ada[16:24],
                             tiles(np.concatenate([A(w_conv_out)[0], w_ao])), tiles(A(w_out)[0]), ada[24:40],
                             tiles(A(w_pq)[0]), ada[40:48]])
    stream = np.ascontiguousarray(stream.reshape(ROUNDS * 4, 2, P, -1).transpose(0, 2, 1, 3).reshape(ROUNDS * 4, P, -1))
    wqkv = tiles(np.concatenate([w_q, w_in[:, 1536:1792]], 1)).reshape(6, P, KT, P).transpose(1, 0, 2, 3)
    col = lambda a: A(a).reshape(-1, P).T
    cols = np.concatenate([col(b_ada), col(g_norm1), col(g_norm2), col(b_dw), col(ln_g), col(ln_b),
                           A(w_dw)[0].T.reshape(CT, P, TAPS).transpose(1, 0, 2).reshape(P, -1), col(c)], 1)
    rows = np.broadcast_to(np.concatenate([A(attn_sinks)[0][pair], A(g_final)])[None], (P, HEADS + D))
    arrays = {
        "stream": stream, "wqkv": wqkv,
        "skT": A(sub_keys)[0].reshape(2 * PH, NK, P).transpose(2, 0, 1),
        "xT": A(x)[0].T.reshape(KT, P, T).transpose(1, 0, 2),
        "cols": cols, "rows": rows, "biasd": slope_bias(), "identd": np.eye(P, dtype=np.float32),
        "pu": A(peer_u)[0], "pv": A(peer_v)[0],
    }
    arrays = {k: np.ascontiguousarray(a) for k, a in arrays.items()}
    nc = _bacc.Bacc("TRN2", target_bir_lowering=False, num_devices=1)
    aps = [nc.dram_tensor(k, a.shape, _mybir.dt.from_np(a.dtype), kind="ExternalInput").ap() for k, a in arrays.items()]
    out = nc.dram_tensor("out", (T, D), _mybir.dt.float32, kind="ExternalOutput").ap()
    build(nc, *aps, out)
    r = _run(nc, [arrays], core_ids=[0])
    return r.results[0]["out"].reshape(1, T, D)
```

```python
import math

import numpy as np
import concourse.bass as bass
from concourse import mybir
from contextlib import ExitStack

P = 128
D = 1024
T = 512
KT = D // P
TB = T // P
CT = 4
TAPS = 31
HEADS = 8
HD = 64
PAIRS = HEADS // 2
KEYS = 256
PH = 8
NK = 128
TOPK = 16
SLOTS = PH * TOPK
ROWBUF = 8
EPS = 1e-6

DB = TB - 1
DT = DB * P
XT = NK
HT = 64
PIECES = DT // HT

R_ADA1, R_CONV, R_ADAG1, R_GATE, R_PROJ, R_WOUT, R_PQ, R_ADAG2, ROUNDS = 0, 2, 3, 4, 8, 9, 10, 12, 13

N_RMS1 = 0
N_CONV = 1
N_QKV = N_CONV + 2 * CT
N_GATE = N_QKV + 6
N_LN = N_GATE + 2 * KT
N_PROJ = N_LN + 2
N_WOUT = N_PROJ + 2 * KT
N_RMS2 = N_WOUT + KT
N_PQ = N_RMS2 + 1
N_TOK = N_PQ + 2 * PH
N_G2 = N_TOK + 2 * TB + 2
N_LIST = N_G2 + 2
BANKS = 4


def build(nc, stream, wqkv, skT, xT, cols, rows, biasd, identd, puT, pu, pv, gmat, out):
    f32, f32r, i32, u32 = mybir.dt.float32, mybir.dt.float32r, mybir.dt.int32, mybir.dt.uint32
    ALU, ACT, AX = mybir.AluOpType, mybir.ActivationFunctionType, mybir.AxisListType
    NEG = -3.0e38

    with ExitStack() as ctx:
        def sb(name, shape, dt=f32):
            return ctx.enter_context(nc.sbuf_tensor(name, shape, dt))

        def sem(name):
            return ctx.enter_context(nc.semaphore(name))

        big = sb("big", [P, 4 * D * 4])
        wring = big[:, 0:8 * D].rearrange("p (s j k c) -> p s j k c", s=4, j=2, k=KT)
        hT = big[:, 8 * D:12 * D].rearrange("p (k t) -> p k t", k=KT)
        nT = big[:, 12 * D:16 * D].rearrange("p (k t) -> p k t", k=KT)
        mid = sb("mid", [P, 6 * D])
        qkvw = mid[:, :].rearrange("p (j k c) -> p j k c", j=6, k=KT)
        low = sb("low", [P, 4 * D])
        skw = low[:, 0:2 * D].rearrange("p (h n) -> p h n", n=NK)
        bias = low[:, 2 * D:4 * D].rearrange("p (h k) -> p h k", k=KEYS)
        colv = sb("colv", [P, 208])
        rowv = sb("rowv", [P, HEADS + D])
        ident = sb("ident", [P, P])
        ones = sb("ones", [P, P])
        eps = sb("eps", [P, 1])
        cond = sb("cond", [P, KT])
        mod = sb("mod", [P, 6 * KT])
        coef = sb("coef", [P, 2, KT])
        sq = sb("sq", [P, 2, T])
        std = sb("std", [P, T])
        rstd = sb("rstd", [P, T])
        nsink = sb("nsink", [P, HEADS])
        attnT = sb("attnT", [P, PAIRS, T])
        vtok = sb("vtok", [P, TB, P])
        att = sb("att", [P, 5 * T])
        ssb = att[:, 0:2 * T].rearrange("p (r e k) -> p r e k", r=2, e=2)
        pexp = att[:, 2 * T:4 * T].rearrange("p (r e k) -> p r e k", r=2, e=2)
        ptsb = sb("ptsb", [P, 2, 4, P])
        nmx = sb("nmx", [P, 2, 2])
        mx = sb("mx", [P, 2, 2])
        rs = sb("rs", [P, 2, 2])
        es = sb("es", [P, 2, 2])
        den = sb("den", [P, 2, 2])
        rden = sb("rden", [P, 2, 2])
        dot1 = sb("dot1", [P, ROWBUF])
        dots = sb("dots", [P, SLOTS])
        act_w = sb("act_w", [P, SLOTS])
        islot = sb("islot", [P, ROWBUF], i32)
        eidx = sb("eidx", [P, SLOTS], i32)
        gsum = sb("gsum", [P, TB * PH])
        iotan = sb("iotan", [P, NK])
        ssum = sb("ssum", [P, TB])
        sstd = sb("sstd", [P, TB])
        srstd = sb("srstd", [P, TB])

        front = ExitStack()
        gates = front.enter_context(nc.sbuf_tensor("gates", [P, 2 * KT, T], f32))
        PADT = T + TAPS - 1
        WORK = CT * PADT + CT * T + 2 * T + PAIRS * T + T
        W = front.enter_context(nc.sbuf_tensor("work", [P, WORK], f32))
        u = W[:, 0:CT * PADT].rearrange("p (m t) -> p m t", m=CT)
        o0 = CT * PADT
        y = W[:, o0:o0 + CT * T].rearrange("p (m t) -> p m t", m=CT)
        o0 += CT * T
        sg = W[:, o0:o0 + 2 * T].rearrange("p (m t) -> p m t", m=2)
        o0 += 2 * T
        qT = W[:, o0:o0 + PAIRS * T].rearrange("p (m t) -> p m t", m=PAIRS)
        o0 += PAIRS * T
        kT = W[:, o0:o0 + T]
        front.close()
        xs = sb("xs", [P, 2, KT, DT], f32r)
        As = sb("As", [P, 2, 2, DT], f32r)
        Us = sb("Us", [P, 2, 2, D], f32r)
        Vs = sb("Vs", [P, 2, 2, D], f32r)

        b_ada, g1, g2 = colv[:, 0:48], colv[:, 48:56], colv[:, 56:64]
        b_dw, ln_g, ln_b = colv[:, 64:68], colv[:, 68:72], colv[:, 72:76]
        w_dw = colv[:, 76:76 + CT * TAPS].rearrange("p (m k) -> p m k", m=CT)
        ccol = colv[:, 200:208]
        gfin = rowv[:, HEADS:HEADS + D]

        Q = mid[:, :]
        qh = Q[:, 0:4 * T].rearrange("p (e s t) -> p e s t", e=2, s=2)
        sc = Q[:, 4 * T:4 * T + 2 * 8 * NK].rearrange("p (e r n) -> p e r n", e=2, r=8)
        o1 = 4 * T + 2 * 8 * NK
        sc2 = Q[:, o1:o1 + 8 * NK].rearrange("p (r n) -> p r n", r=8)
        o1 += 8 * NK
        cand = Q[:, o1:o1 + TB * 256].rearrange("p (b n) -> p b n", b=TB)
        assert o1 + TB * 256 <= 6 * KT * P
        cand2 = low[:, 2 * D:3 * D].rearrange("p (b n) -> p b n", b=TB)
        hot = low[:, 3 * D:4 * D].rearrange("p (b k a) -> p b k a", b=TB, k=TOPK)
        A4 = attnT[:, :, :].rearrange("p m (b h k) -> p m b h k", h=PH, k=TOPK)
        bests, gw, isel, jsel = (A4[:, q] for q in range(4))
        eight = lambda o: att[:, o:o + TB * 2 * TOPK]
        vals, vidx = (eight(o).rearrange("p (b s k) -> p b s k", b=TB, s=2) for o in (0, 128))
        vidf = [eight(o).rearrange("p (b s k) -> p b s k", b=TB, s=2) for o in (256, 384)]
        posf = [eight(o).rearrange("p (s b k) -> p s b k", b=TB, s=2) for o in (512, 640)]
        posa = eight(768).rearrange("p (s b k) -> p s b k", b=TB, s=2)
        best, pos, sel = (att[:, o:o + TB * TOPK].rearrange("p (b k) -> p b k", b=TB) for o in (896, 960, 1024))
        vidx, posa, pos = vidx.bitcast(u32), posa.bitcast(u32), pos.bitcast(u32)
        iota16 = iotan[:, 0:TOPK]
        diag = sq[:, :, :].rearrange("p a (q c) -> p (a q) c", c=P)

        h_tok = mid[:, 0:4 * D].rearrange("p (b d) -> p b d", b=TB)
        n_tok = mid[:, 4 * D:5 * D]
        g2row = mid[:, 5 * D:6 * D]

        piece = big[:, :].rearrange("p (a i t) -> p a i t", a=2, i=NK)
        ohj = low[:, 0:2 * D].rearrange("p (s j) -> p s j", j=NK)
        ohi = low[:, 2 * D:4 * D].rearrange("p (s j) -> p s j", j=NK)
        lists = att[:, 0:3 * DT].rearrange("p (q t) -> p q t", q=3)

        uraw = big[:, 0:4 * D].rearrange("p (s a f) -> p s a f", s=2, a=2)
        vraw = big[:, 4 * D:8 * D].rearrange("p (s a f) -> p s a f", s=2, a=2)
        row = big[:, 8 * D:16 * D].rearrange("p (s f) -> p s f", f=D)
        acc = low[:, 0:2 * D].rearrange("p (a d) -> p a d", a=2)
        yout = low[:, 2 * D:4 * D].rearrange("p (a d) -> p a d", a=2)
        graw = att[:, 0:4 * DT].rearrange("p (s h a t) -> p s h a t", s=2, h=PIECES, a=2)
        gel = att[:, 4 * DT:6 * DT].rearrange("p (s t) -> p s t", s=2)

        ps = ctx.enter_context(nc.psum_tensor("ps", [P, 8, 512], f32))
        PT_B, O_B = ps[:, 6, :], ps[:, 7, :]
        MOD = ps[:, 7, 0:6 * KT]

        small_here = sem("small_here")
        x_here = sem("x_here")
        qkvw_here = sem("qkvw_here")
        late_here = sem("late_here")
        out_done = [sem(f"out_done{e}") for e in range(2)]
        w_here = [sem(f"w_here{s}") for s in range(4)]
        pair_begun = sem("pair_begun")
        consts = sem("consts")
        cond_ready = sem("cond_ready")
        tile_done = sem("tile_done")
        bank_free = [sem(f"bank_free{b}") for b in range(BANKS)]
        mod_done = sem("mod_done")
        mod_ready = sem("mod_ready")
        sq_ready, sq_used = sem("sq_ready"), sem("sq_used")
        scaled = sem("scaled")
        n_ready = sem("n_ready")
        s_done, s_biased = sem("s_done"), sem("s_biased")
        nmx_ready, exp_done, p_ready = sem("nmx_ready"), sem("exp_done"), sem("p_ready")
        pt_done, pt_ready = sem("pt_done"), sem("pt_ready")
        o_done, o_ready = sem("o_done"), sem("o_ready")
        dve_step = sem("dve_step")
        dve_turn = sem("dve_turn")
        y_ready, yc_ready, yn_ready, silu_ready = sem("y_ready"), sem("yc_ready"), sem("yn_ready"), sem("silu_ready")
        merged = sem("merged")
        sc_done, sc_ready, sc_free = sem("sc_done"), sem("sc_ready"), sem("sc_free")
        pos_ready, sel_free = sem("pos_ready"), sem("sel_free")
        pool_step = sem("pool_step")
        sm_in, sm_exp = sem("sm_in"), sem("sm_exp")
        list_in = sem("list_in")
        xhi_ready, xlo_ready = sem("xhi_ready"), sem("xlo_ready")
        oh_ready, oh_used, g_taken = sem("oh_ready"), sem("oh_used"), sem("g_taken")
        piece_out, piece_free = sem("piece_out"), sem("piece_free")
        u_here, v_here, g_here = ([sem(f"{w}_here{e}") for e in range(2)] for w in "uvg")
        uhi_ready, ulo_ready, vhi_ready, vlo_ready = (sem(f"{w}_ready") for w in ("uhi", "ulo", "vhi", "vlo"))
        u_done, v_done = sem("u_done"), sem("v_done")
        gel_ready, a_ready, ahi_ready, alo_ready = (sem(f"{w}_ready") for w in ("gel", "a", "ahi", "alo"))
        idx_ready = sem("idx_ready")
        slot_copied, pool_turn = sem("slot_copied"), sem("pool_turn")
        row_here = [sem(f"row_here{b}") for b in range(ROWBUF)]
        row_used = sem("row_used")
        dots_ready, gelu_ready = sem("dots_ready"), sem("gelu_ready")
        y_sum, y_sq, y_std, y_out = sem("y_sum"), sem("y_sq"), sem("y_std"), sem("y_out")

        def freed(eng, n):
            eng.wait_ge(bank_free[n % BANKS], n // BANKS + 1)

        block = ctx.enter_context(nc.Block())

        @block.sync
        def _(sp):
            sp.dma_start(colv[:, :], cols).then_inc(small_here, 16)
            sp.dma_start(hT[:, :, :], xT).then_inc(x_here, 16)

            def load_round(r, wait):
                for s in range(4):
                    if wait:
                        sp.wait_ge(pair_begun, r * 4 + s - 2)
                    sp.dma_start(wring[:, s, :, :, :].rearrange("p a b c -> p (a b c)"),
                                 stream[bass.ds(r * 4 + s, 1), :, :].rearrange("a p f -> (a p) f")
                                 ).then_inc(w_here[s], 16)
            load_round(0, False)
            sp.dma_start(ident[:, :], identd).then_inc(late_here, 16)
            sp.dma_start(rowv[:, :], rows).then_inc(late_here, 16)
            load_round(1, True)
            load_round(2, True)
            sp.dma_start(mid[:, :], wqkv).then_inc(qkvw_here, 16)
            sp.dma_start(bias, biasd).then_inc(late_here, 16)
            sp.dma_start(skw, skT).then_inc(late_here, 16)
            with sp.Fori(3, ROUNDS) as r:
                load_round(r, True)

            with sp.Fori(0, DB) as b:
                for e in range(2):
                    sp.wait_ge(g_taken, b * 32 + 16 * (e + 1) + 4)
                    sp.dma_start(gmat[bass.ds(b * 2 + e, 1), :, :].rearrange("a p f -> (a p) f"),
                                 piece[:, e, :, :].rearrange("p i t -> p (i t)")).then_inc(piece_out, 16)
                    sp.wait_ge(piece_out, b * 32 + 16 * (e + 1))
                    sp.sem_inc(piece_free, 1)

            def load_experts(g, first):
                for e in range(2):
                    q = g * 2 + e
                    if not first:
                        sp.wait_ge(ulo_ready, q * 2 - 2)
                    sp.dma_start(uraw[:, e, :, :].rearrange("p a f -> p (a f)"),
                                 puT[bass.ds(q, 1), :, :].rearrange("a p f -> (a p) f")).then_inc(u_here[e], 16)
                    if not first:
                        sp.wait_ge(a_ready, q * 2 - 2)
                    sp.dma_start(graw[:, e, :, :, :].rearrange("p h a t -> p h (a t)"),
                                 gmat[:, :, bass.ds(q * 2 * HT, 2 * HT)].rearrange("h p f -> p h f")
                                 ).then_inc(g_here[e], 16)
                    if not first:
                        sp.wait_ge(vlo_ready, q * 2 - 2)
                    sp.dma_start(vraw[:, e, :, :],
                                 pv[bass.ds(q * 2 * P, 2 * P), :].rearrange("(a p) f -> p a f", p=P)
                                 ).then_inc(v_here[e], 16)
            load_experts(0, True)
            with sp.Fori(1, XT // 4) as g:
                load_experts(g, False)
            for b in range(TB):
                sp.wait_ge(y_out, b + 1)
                sp.dma_start(out[b * P:(b + 1) * P, :], yout[:, b % 2, :]).then_inc(out_done[b % 2], 16)
            for e in range(2):
                sp.wait_ge(out_done[e], 16 * TB // 2)

        @block.gpsimd
        def _(pool):
            nc.gpsimd.memset(ones[:, :], 1.0).then_inc(consts, 1)
            nc.gpsimd.memset(eps[:, :], EPS).then_inc(consts, 1)
            nc.gpsimd.memset(u[:, :, 0:TAPS - 1], 0.0).then_inc(consts, 1)
            nc.gpsimd.iota(iotan[:, :], pattern=[[1, NK]], base=0, channel_multiplier=0,
                           allow_small_or_imprecise_dtypes=True).then_inc(consts, 1)

            for k in range(KT):
                pool.wait_ge(xhi_ready, k + 1)
                nc.gpsimd.tensor_tensor(xs[:, 1, k, :], nT[:, k, P:T], xs[:, 0, k, :].bitcast(f32), ALU.subtract
                                        ).then_inc(xlo_ready, 1)

            hotv = hot.rearrange("p b k a -> p (b k) a")
            nc.gpsimd.sem_inc(sel_free, 2)
            pool.wait_ge(consts, 4)
            STEPS = 13
            with pool.Fori(0, PH // 2) as h2:
                for e in range(2):
                    n = [e * STEPS]
                    h = h2 * 2 + e

                    def pstep(ins):
                        n[0] += 1
                        ins.then_inc(pool_step, 1)
                        pool.wait_ge(pool_step, h2 * (2 * STEPS) + n[0])
                        nc.gpsimd.sem_inc(pool_turn, 1)

                    pool.wait_ge(pos_ready, h + 1)
                    for half, dst in enumerate((isel, jsel)):
                        pstep(nc.gpsimd.tensor_tensor(
                            hotv, posf[e][:, half, :, :].rearrange("p b k -> p (b k)").unsqueeze(2)
                            .broadcast_to([P, TB * TOPK, TOPK]),
                            iota16.unsqueeze(1).broadcast_to([P, TB * TOPK, TOPK]), ALU.subtract))
                        pstep(nc.gpsimd.tensor_scalar(hotv, hotv, 0.0, None, ALU.is_equal))
                        pstep(nc.gpsimd.tensor_tensor(hot, hot, vidf[e][:, :, half, :].unsqueeze(2)
                                                      .broadcast_to([P, TB, TOPK, TOPK]), ALU.mult))
                        for w in (8, 4, 2):
                            pstep(nc.gpsimd.tensor_tensor(hot[:, :, :, 0:w], hot[:, :, :, 0:w], hot[:, :, :, w:2 * w],
                                                          ALU.add))
                        i = nc.gpsimd.tensor_tensor(dst[:, :, bass.ds(h, 1), :].rearrange("p b a k -> p b (a k)"),
                                                    hot[:, :, :, 0], hot[:, :, :, 1], ALU.add)
                        if half == 0:
                            pstep(i)
                        else:
                            i.then_inc(sel_free, 1)
                            pool.wait_ge(sel_free, h + 3)
                            nc.gpsimd.sem_inc(pool_turn, 1)

            def fetch(table, k0, r0, wait):
                for s in range(ROWBUF):
                    if wait:
                        pool.wait_ge(row_used, k0 + (r0 - ROWBUF + s + 1))
                    nc.gpsimd.tensor_copy(islot[:, s:s + 1], eidx[:, bass.ds(k0 + s, 1)]).then_inc(slot_copied, 1)
                    pool.wait_ge(slot_copied, k0 + (r0 + s + 1))
                    nc.gpsimd.sem_inc(pool_turn, 1)
                    nc.gpsimd.indirect_dma_start(
                        out=row[:, s, :], out_offset=None, in_=table,
                        in_offset=bass.IndirectOffsetOnAxis(ap=islot[:, s:s + 1], axis=0)).then_inc(row_here[s], 16)
            pool.wait_ge(idx_ready, 1)
            pool.wait_ge(piece_out, 16 * PIECES)
            fetch(pu, 0, 0, False)
            with pool.Fori(1, SLOTS // ROWBUF) as group:
                fetch(pu, group * ROWBUF, 0, True)
            with pool.Fori(0, SLOTS // ROWBUF) as group:
                fetch(pv, group * ROWBUF, SLOTS, True)

        @block.tensor
        def _(pe):
            def bank(n):
                if n >= BANKS:
                    pe.wait_ge(bank_free[n % BANKS], n // BANKS)
                return ps[:, n % BANKS, :]

            def column_sums(n, sq0, count):
                o = bank(n)
                for k in range(count):
                    pe.wait_ge(sq_ready, sq0 + k + 1)
                    mm = nc.tensor.matmul(o, ones[:, :], sq[:, (sq0 + k) % 2, :], start=(k == 0), stop=(k == count - 1))
                    mm.then_inc(sq_used if k < count - 1 else tile_done, 1)

            def ada(r, tile0):
                for s in range(4):
                    pe.wait_ge(w_here[s], (r + 1) * 16)
                    for j in range(2):
                        for k in range(KT):
                            mm = nc.tensor.matmul(MOD[:, bass.ds(tile0 + 2 * s + j, 1)],
                                                  wring[:, s, j, k, :], cond[:, k:k + 1],
                                                  start=(k == 0), stop=(k == KT - 1))
                            if j + k == 0:
                                mm.then_inc(pair_begun, 1)
                return mm

            def product(o, lhs, rhs, count=KT, begins=False):
                for k in range(count):
                    mm = nc.tensor.matmul(o, lhs(k), rhs(k), start=(k == 0), stop=(k == count - 1))
                    if begins and k == 0:
                        mm.then_inc(pair_begun, 1)
                return mm

            pe.wait_ge(consts, 1)
            column_sums(N_RMS1, 0, KT)
            pe.wait_ge(cond_ready, 1)
            ada(0, 0)
            ada(1, KT).then_inc(mod_done, 1)

            pe.wait_ge(n_ready, KT)
            for s in range(4):
                pe.wait_ge(w_here[s], (R_CONV + 1) * 16)
                for j in range(2):
                    mm = product(bank(N_CONV + 2 * s + j), lambda k: wring[:, s, j, k, :], lambda k: nT[:, k, :], begins=j == 0)
                    mm.then_inc(tile_done, 1)

            pe.wait_ge(qkvw_here, 16)
            for j in range(5):
                mm = product(bank(N_QKV + j), lambda k: qkvw[:, j, k, :], lambda k: nT[:, k, :])
                mm.then_inc(tile_done, 1)
            o = bank(N_QKV + 5)
            for b in range(TB):
                mm = product(o[:, b * P:(b + 1) * P], lambda k: nT[:, k, b * P:(b + 1) * P], lambda k: qkvw[:, 5, k, :])
            mm.then_inc(tile_done, 1)

            for j in range(2, 6):
                freed(pe, N_QKV + j)
            pe.wait_ge(late_here, 64)

            def att_scores(a):
                b, m = divmod(a, PAIRS)
                if a >= 2:
                    pe.wait_ge(s_biased, a - 1)
                k0, c0 = (0, P) if b == 0 else ((b - 1) * P, 0)
                for e in range(2):
                    mm = nc.tensor.matmul(ps[:, 2 * (a % 2) + e, c0:KEYS], qT[e * HD:(e + 1) * HD, m, b * P:(b + 1) * P],
                                          kT[e * HD:(e + 1) * HD, k0:(b + 1) * P], start=True, stop=True)
                mm.then_inc(s_done, 1)

            def att_out(a):
                b, m = divmod(a, PAIRS)
                tiles = (1,) if b == 0 else (0, 1)
                pe.wait_ge(p_ready, a + 1)
                if a >= 1:
                    pe.wait_ge(pt_ready, a)
                for e in range(2):
                    for c in tiles:
                        mm = nc.tensor.transpose(PT_B[:, (2 * e + c) * P:(2 * e + c + 1) * P],
                                                 pexp[:, a % 2, e, c * P:(c + 1) * P], ident[:, :])
                mm.then_inc(pt_done, 1)
                if a + 2 < TB * PAIRS:
                    att_scores(a + 2)
                pe.wait_ge(pt_ready, a + 1)
                if m == 0 and b >= 1:
                    pe.wait_ge(o_ready, b)
                for e in range(2):
                    for c in tiles:
                        mm = nc.tensor.matmul(O_B[e * HD:(e + 1) * HD, m * P:(m + 1) * P],
                                              vtok[:, b - 1 + c, e * HD:(e + 1) * HD], ptsb[:, a % 2, 2 * e + c, :],
                                              start=(c == tiles[0]), stop=(c == 1))
                if m == PAIRS - 1:
                    mm.then_inc(o_done, 1)

            att_scores(0)
            att_scores(1)
            for a in range(TB * PAIRS):
                att_out(a)

            pe.wait_ge(o_ready, TB)
            ada(R_ADAG1, 2 * KT)

            pe.wait_ge(s_biased, TB * PAIRS)
            with pe.Fori(0, 2) as r:
                for s in range(4):
                    pe.wait_ge(w_here[s], (r * 2 + R_GATE + 1) * 16)
                    for j in range(2):
                        n0 = N_GATE + 2 * s + j
                        pe.wait_ge(bank_free[n0 % BANKS], r * 2 + n0 // BANKS)
                        mm = product(ps[:, n0 % BANKS, :], lambda k: wring[:, s, j, k, :], lambda k: nT[:, k, :], begins=j == 0)
                        mm.then_inc(tile_done, 1)

                ada(r * 2 + (R_GATE + 1), r * KT + 3 * KT).then_inc(mod_done, 1)

            o = bank(N_LN)
            pe.wait_ge(y_ready, CT)
            mm = product(o, lambda k: ones[:, :], lambda k: y[:, k, :], CT)
            mm.then_inc(tile_done, 1)
            column_sums(N_LN + 1, KT, CT)

            pe.wait_ge(silu_ready, CT)
            for s in range(4):
                pe.wait_ge(w_here[s], (R_PROJ + 1) * 16)
                for j in range(2):
                    n = N_PROJ + 4 * s + 2 * j
                    mm = product(bank(n), lambda k: wring[:, s, j, k, :], lambda k: y[:, k, :], CT, begins=j == 0)
                    mm.then_inc(tile_done, 1)
                    mm = product(bank(n + 1), lambda k: wring[:, s, j, CT + k, :], lambda k: attnT[:, k, :], CT)
                    mm.then_inc(tile_done, 1)

            pe.wait_ge(merged, KT)
            for s in range(4):
                pe.wait_ge(w_here[s], (R_WOUT + 1) * 16)
                for j in range(2):
                    mm = product(bank(N_WOUT + 2 * s + j), lambda k: wring[:, s, j, k, :], lambda k: gates[:, k, :],
                                 begins=j == 0)
                    mm.then_inc(tile_done, 1)

            column_sums(N_RMS2, KT + CT, KT)
            pe.wait_ge(n_ready, 2 * KT)

            with pe.Fori(0, 2) as r:
                for s in range(4):
                    pe.wait_ge(w_here[s], (r + R_PQ + 1) * 16)
                    for j in range(2):
                        n0 = N_PQ + 2 * s + j
                        pe.wait_ge(bank_free[n0 % BANKS], r * 2 + n0 // BANKS)
                        mm = product(ps[:, n0 % BANKS, :], lambda k: wring[:, s, j, k, :], lambda k: nT[:, k, :], begins=j == 0)
                        mm.then_inc(tile_done, 1)
                    pe.wait_ge(bank_free[(N_PQ + 2 * s) % BANKS], r * 2 + (N_PQ + 2 * s) // BANKS + 1)
                    pe.wait_ge(bank_free[(N_PQ + 2 * s + 1) % BANKS], r * 2 + (N_PQ + 2 * s + 1) // BANKS + 1)
                    pe.wait_ge(sc_ready, r * 4 + s + 1)
                    for b in range(TB):
                        for half in range(2):
                            mm = nc.tensor.matmul(
                                ps[:, 4 + b // 2, ((b % 2) * 2 + half) * NK:((b % 2) * 2 + half + 1) * NK],
                                qh[:, s % 2, half, b * P:(b + 1) * P],
                                skw[:, bass.ds(r * 8 + 2 * s + half, 1), :].rearrange("p a n -> p (a n)"),
                                start=True, stop=True)
                    mm.then_inc(sc_done, 1)

            pe.wait_ge(mod_ready, 3)
            ada(R_ADAG2, 5 * KT).then_inc(mod_done, 1)

            for w in range(2 * TB + 2):
                b, half = divmod(w, 2)
                src, b = (hT, b) if b < TB else (nT, 0)
                o = bank(N_TOK + w)
                for q in range(4):
                    mm = nc.tensor.transpose(o[:, q * P:(q + 1) * P], src[:, 4 * half + q, b * P:(b + 1) * P],
                                             ident[:, :])
                mm.then_inc(tile_done, 1)
            pe.wait_ge(mod_ready, 5)
            for half in range(2):
                o = bank(N_G2 + half)
                for q in range(4):
                    mm = nc.tensor.matmul(o[:, q * P:(q + 1) * P], ones[:, :], diag[:, 4 * half + q, :],
                                          start=True, stop=True)
                mm.then_inc(tile_done, 1)
            pe.wait_ge(list_in, 1)
            for q, src in enumerate((isel, jsel, gw)):
                o = bank(N_LIST + q)
                for b in range(DB):
                    mm = nc.tensor.transpose(o[:, b * P:(b + 1) * P],
                                             src[:, b + 1, :, :].rearrange("p h k -> p (h k)"), ident[:, :])
                mm.then_inc(tile_done, 1)

            for q in range(3):
                freed(pe, N_LIST + q)
            nc.tensor.sem_inc(oh_used, 4)
            with pe.Fori(0, PIECES * 4) as it:
                for c in range(4):
                    pe.wait_ge(oh_ready, it * 4 + c + 1)
                    pe.wait_ge(g_taken, it * 4 + c + 1)
                    for t in range(4):
                        mm = nc.tensor.matmul(ps[:, c, t * P:(t + 1) * P], ohj[:, 4 * c + t, :], ohi[:, 4 * c + t, :],
                                              start=True, stop=True)
                    mm.then_inc(oh_used, 1)

            def hidden(n, e, first):
                pe.wait_ge(ulo_ready, n + 1)
                if not first:
                    pe.wait_ge(gel_ready, n - 1)
                for k in range(KT):
                    hi, lo = (Us[:, e, w, k * P:(k + 1) * P] for w in range(2))
                    for a, b in ((hi, 0), (hi, 1), (lo, 0)):
                        mm = nc.tensor.matmul(ps[:, 6 + e, 0:DT], a, xs[:, b, k, :],
                                              start=(k == 0 and a is hi and b == 0), stop=(k == KT - 1 and a is lo))
                mm.then_inc(u_done, 1)

            def output(n, e, first=False, last=False):
                pe.wait_ge(alo_ready, n + 1)
                pe.wait_ge(vlo_ready, n + 1)
                for b in range(DB):
                    hi, lo = (As[:, e, w, b * P:(b + 1) * P] for w in range(2))
                    for a, w in ((hi, 0), (hi, 1), (lo, 0)):
                        for half in range(2):
                            mm = nc.tensor.matmul(ps[:, 2 * b + half, :], a, Vs[:, e, w, half * T:(half + 1) * T],
                                                  start=(first and a is hi and w == 0), stop=(last and a is lo))
                mm.then_inc(v_done, 1)

            pe.wait_ge(xlo_ready, KT)
            pe.wait_ge(g_taken, PIECES * 16 + 4)
            for n in range(4):
                hidden(n, n % 2, n < 2)
                if n:
                    output(n - 1, (n - 1) % 2, first=n == 1)
            with pe.Fori(1, XT // 4) as g:
                for c in range(4):
                    hidden(g * 4 + c, c % 2, False)
                    output(g * 4 + (c - 1), (c - 1) % 2)
            output(XT - 1, (XT - 1) % 2, last=True)

        @block.scalar
        def _(act):
            f = nc.scalar.activation
            act.wait_ge(small_here, 16)
            f(cond[:, :], ccol, ACT.Silu).then_inc(cond_ready, 1)

            def squares(src, n0, used, count, need):
                for k in range(count):
                    need(k)
                    if k >= 2:
                        act.wait_ge(sq_used, used + k - 1)
                    f(sq[:, (n0 + k) % 2, :], src(k), ACT.Square).then_inc(sq_ready, 1)

            def root(n, count):
                act.wait_ge(tile_done, n + 1)
                f(std[:, :], ps[:, n % BANKS, :], ACT.Sqrt, bias=eps[:, 0:1], scale=1.0 / count
                  ).then_inc(bank_free[n % BANKS], 1)

            def modulate(stage, shift0):
                for k in range(KT):
                    act.wait_ge(scaled, stage * KT + k + 1)
                    f(nT[:, k, :], nT[:, k, :], ACT.Identity, scale=coef[:, stage, k:k + 1],
                      bias=mod[:, shift0 + k:shift0 + k + 1]).then_inc(n_ready, 1)

            act.wait_ge(x_here, 16)
            squares(lambda k: hT[:, k, :], 0, 0, KT, lambda k: None)
            act.wait_ge(consts, 3)
            root(N_RMS1, D)
            act.wait_ge(mod_ready, 1)
            modulate(0, 0)

            for m in range(CT):
                n = N_CONV + 2 * m + 1
                act.wait_ge(tile_done, n + 1)
                if m >= 2:
                    freed(act, n - 5)
                f(sg[:, m % 2, :], ps[:, n % BANKS, :], ACT.Sigmoid).then_inc(bank_free[n % BANKS], 1)
            for j in range(6):
                n = N_QKV + j
                act.wait_ge(tile_done, n + 1)
                dst = (qT[:, j, :] if j < 4 else kT[:, :] if j == 4 else
                       vtok[:, :, :].rearrange("p b d -> p (b d)"))
                f(dst, ps[:, n % BANKS, :], ACT.Copy, scale=HD ** -0.5 if j < 4 else 1.0
                  ).then_inc(bank_free[n % BANKS], 1)

            def att_evac(a):
                b = a // PAIRS
                act.wait_ge(pt_done, a + 1)
                s0 = P if b == 0 else 0
                view = lambda t: t.rearrange("p (e k) -> p e k", e=2)[:, :, s0:KEYS]
                f(view(ptsb[:, a % 2, :, :].rearrange("p c q -> p (c q)")), view(PT_B), ACT.Copy).then_inc(pt_ready, 1)
                if a % PAIRS == PAIRS - 1:
                    act.wait_ge(o_done, b + 1)
                    f(attnT[:, :, b * P:(b + 1) * P], O_B.rearrange("p (m q) -> p m q", m=PAIRS), ACT.Copy
                      ).then_inc(o_ready, 1)
            for a in range(TB * PAIRS):
                c0 = P if a < PAIRS else 0
                act.wait_ge(nmx_ready, a + 1)
                if a >= 2:
                    act.wait_ge(pt_done, a - 1)
                for e in range(2):
                    f(pexp[:, a % 2, e, c0:KEYS], ssb[:, a % 2, e, c0:KEYS], ACT.Exp, bias=nmx[:, a % 2, e:e + 1],
                      accum_out=rs[:, a % 2, e:e + 1])
                f(es[:, a % 2, :], mx[:, a % 2, :], ACT.Exp).then_inc(exp_done, 1)
                if a >= 1:
                    att_evac(a - 1)
            att_evac(TB * PAIRS - 1)

            with act.Fori(0, 2 * KT // 4) as t4:
                t = t4 * 4
                for j in range(4):
                    act.wait_ge(tile_done, t + N_GATE + j + 1)
                    f(gates[:, bass.ds(t + j, 1), :].rearrange("p a t -> p (a t)"),
                      ps[:, (N_GATE + j) % BANKS, :], ACT.Sigmoid).then_inc(bank_free[(N_GATE + j) % BANKS], 1)

            squares(lambda k: y[:, k, :], KT, KT - 1, CT, lambda k: act.wait_ge(yc_ready, k + 1))
            root(N_LN + 1, CT * P)
            for m in range(CT):
                act.wait_ge(yn_ready, m + 1)
                f(y[:, m, :], y[:, m, :], ACT.Silu, scale=ln_g[:, m:m + 1], bias=ln_b[:, m:m + 1]).then_inc(silu_ready, 1)

            squares(lambda k: hT[:, k, :], KT + CT, KT + CT - 2, KT, lambda k: freed(act, N_WOUT + k))
            root(N_RMS2, D)
            act.wait_ge(mod_ready, 3)
            modulate(1, 3 * KT)


            for k in range(KT):
                act.wait_ge(n_ready, KT + k + 1)
                f(xs[:, 0, k, :], nT[:, k, P:T], ACT.Copy).then_inc(xhi_ready, 1)

            nc.scalar.sem_inc(sc_ready, 1)
            nc.scalar.sem_inc(sc_free, 2)
            with act.Fori(0, PH // 2) as h2:
                h = h2 * 2
                for e in range(2):
                    for half in range(2):
                        n0 = N_PQ + 2 * e + half
                        act.wait_ge(tile_done, h * 2 + n0 + 1)
                        f(qh[:, e, half, :], ps[:, n0 % BANKS, :], ACT.Copy).then_inc(bank_free[n0 % BANKS], 1)
                    act.wait_ge(sc_done, h + e + 1)
                    act.wait_ge(sc_free, h + e + 1)
                    for c in range(2):
                        i = f(sc[:, e, 4 * c:4 * c + 4, :].rearrange("p r n -> p (r n)"), ps[:, 4 + c, :], ACT.Copy)
                    i.then_inc(sc_ready, 1)

            act.wait_ge(sm_in, 1)
            f(gw[:, :, :, :], gw[:, :, :, :], ACT.Exp).then_inc(sm_exp, 1)
            for w in range(2 * TB + 2):
                n = N_TOK + w
                act.wait_ge(tile_done, n + 1)
                f(mid[:, w * T:(w + 1) * T], ps[:, n % BANKS, :], ACT.Copy).then_inc(bank_free[n % BANKS], 1)
            for half in range(2):
                n = N_G2 + half
                act.wait_ge(tile_done, n + 1)
                f(g2row[:, half * T:(half + 1) * T], ps[:, n % BANKS, :], ACT.Copy).then_inc(bank_free[n % BANKS], 1)
            for q in range(3):
                n = N_LIST + q
                act.wait_ge(tile_done, n + 1)
                f(lists[:, q, :], ps[:, n % BANKS, 0:DT], ACT.Copy).then_inc(bank_free[n % BANKS], 1)

            act.wait_ge(xlo_ready, KT)
            nc.scalar.sem_inc(g_taken, 4)
            nc.scalar.sem_inc(piece_free, 2)
            with act.Fori(0, DB) as b:
                for e in range(2):
                    act.wait_ge(piece_free, b * 2 + e + 1)
                    with act.Fori(0, 4) as q:
                        for c in range(4):
                            act.wait_ge(oh_used, b * 32 + q * 4 + (16 * e + c + 1 + 4))
                            f(piece[:, e, :, bass.ds(q * 16 + 4 * c, 4)].rearrange("p i t -> p t i"),
                              ps[:, c, :].rearrange("p (t i) -> p t i", t=4), ACT.Copy).then_inc(g_taken, 1)

            def round_u(n, slot, a, g, first):
                act.wait_ge(u_here[slot], (g + 1) * 16)
                if not first:
                    act.wait_ge(u_done, n - 1)
                f(Us[:, a, 0, :], uraw[:, slot, a, :], ACT.Copy).then_inc(uhi_ready, 1)

            def take(n, slot, a, g, first):
                act.wait_ge(u_done, n + 1)
                if not first:
                    act.wait_ge(alo_ready, n - 1)
                f(gel[:, a, :], ps[:, 6 + a, 0:DT], ACT.Gelu).then_inc(gel_ready, 1)
                act.wait_ge(v_here[slot], (g + 1) * 16)
                if not first:
                    act.wait_ge(v_done, n - 1)
                f(Vs[:, a, 0, :], vraw[:, slot, a, :], ACT.Copy).then_inc(vhi_ready, 1)

            for n in range(4):
                round_u(n, n // 2, n % 2, 0, n < 2)
                if n:
                    take(n - 1, (n - 1) // 2, (n - 1) % 2, 0, n <= 2)
            def dense_steps(g):
                for c in range(4):
                    round_u(g * 4 + c, c // 2, c % 2, g, False)
                    m = (c - 1) % 4
                    take(g * 4 + (c - 1), m // 2, m % 2, g - 1 if c == 0 else g, False)
            with act.Fori(1, XT // 8 + 1) as g:
                dense_steps(g)
            act.wait_ge(dots_ready, SLOTS // ROWBUF)
            f(act_w[:, :], dots[:, :], ACT.Gelu).then_inc(gelu_ready, 1)
            with act.Fori(XT // 8 + 1, XT // 4) as g:
                dense_steps(g)
            take(XT - 1, 1, 1, XT // 4 - 1, False)

            for b in range(TB):
                act.wait_ge(y_sum, b + 1)
                f(row[:, 0, :], yout[:, b % 2, :], ACT.Square, accum_out=ssum[:, b:b + 1]).then_inc(y_sq, 1)
                act.wait_ge(y_sq, b + 1)
                f(sstd[:, b:b + 1], ssum[:, b:b + 1], ACT.Sqrt, bias=eps[:, 0:1], scale=1.0 / D).then_inc(y_std, 1)

        @block.vector
        def _(dve):
            v = nc.vector
            count = [0]

            def step(ins):
                count[0] += 1
                ins.then_inc(dve_step, 1)

            def settled():
                dve.wait_ge(dve_step, count[0])

            def scale_rows(stage):
                n = N_RMS2 if stage else N_RMS1
                freed(dve, n)
                step(v.reciprocal(rstd[:, :], std[:, :]))
                settled()
                for k in range(KT):
                    if stage and k == 0:
                        dve.wait_ge(tile_done, N_GATE + 2 * KT)
                    v.tensor_tensor(nT[:, k, :], hT[:, k, :], rstd[:, :], ALU.mult).then_inc(scaled, 1)

            def take_mod(done, c0, c1):
                dve.wait_ge(mod_done, done)
                return v.tensor_tensor(mod[:, c0:c1], MOD[:, c0:c1], b_ada[:, c0:c1], ALU.add)

            dve.wait_ge(x_here, 16)
            scale_rows(0)
            dve.wait_ge(small_here, 16)
            step(take_mod(1, 0, 2 * KT))
            settled()
            v.scalar_tensor_tensor(coef[:, 0, :], mod[:, KT:2 * KT], 1.0, g1, ALU.add, ALU.mult).then_inc(mod_ready, 1)

            dve.wait_ge(consts, 4)
            for m in range(CT):
                n = N_CONV + 2 * m
                dve.wait_ge(tile_done, n + 1)
                freed(dve, n + 1)
                v.tensor_tensor(u[:, m, TAPS - 1:PADT], ps[:, n % BANKS, :], sg[:, m % 2, :], ALU.mult
                                ).then_inc(bank_free[n % BANKS], 1)

            dve.wait_ge(late_here, 64)
            step(v.tensor_scalar(nsink[:, :], rowv[:, 0:HEADS], -1.0, None, ALU.mult))
            settled()

            def att_norm(a):
                c0 = P if a < PAIRS else 0
                dve.wait_ge(exp_done, a + 1)
                step(v.tensor_tensor(den[:, a % 2, :], rs[:, a % 2, :], es[:, a % 2, :], ALU.add))
                settled()
                step(v.reciprocal(rden[:, a % 2, :], den[:, a % 2, :]))
                settled()
                for e in range(2):
                    i = v.tensor_scalar(pexp[:, a % 2, e, c0:KEYS], pexp[:, a % 2, e, c0:KEYS],
                                        rden[:, a % 2, e:e + 1], None, ALU.mult)
                i.then_inc(p_ready, 1)

            for a in range(TB * PAIRS):
                m = a % PAIRS
                c0 = P if a < PAIRS else 0
                S = ps[:, 2 * (a % 2):2 * (a % 2) + 2, :]
                dve.wait_ge(s_done, a + 1)
                if a >= 2:
                    dve.wait_ge(exp_done, a - 1)
                v.tensor_tensor(ssb[:, a % 2, :, c0:KEYS], S[:, :, c0:KEYS], bias[:, 2 * m:2 * m + 2, c0:KEYS],
                                ALU.add).then_inc(s_biased, 1)
                dve.wait_ge(s_biased, a + 1)
                step(v.tensor_reduce(mx[:, a % 2, :], ssb[:, a % 2, :, c0:KEYS], axis=AX.X, op=ALU.max))
                settled()
                step(v.scalar_tensor_tensor(nmx[:, a % 2, :], mx[:, a % 2, :], -1.0, nsink[:, 2 * m:2 * m + 2],
                                            ALU.mult, ALU.min))
                settled()
                v.tensor_tensor(mx[:, a % 2, :], nmx[:, a % 2, :], nsink[:, 2 * m:2 * m + 2], ALU.subtract
                                ).then_inc(nmx_ready, 1)
                if a >= 1:
                    att_norm(a - 1)
            att_norm(TB * PAIRS - 1)

            for k in range(TAPS):
                base = count[0]
                for m in range(CT):
                    if k == 0:
                        i = v.tensor_scalar(y[:, m, :], u[:, m, 0:T], w_dw[:, m, 0:1], b_dw[:, m:m + 1],
                                            ALU.mult, ALU.add)
                    else:
                        dve.wait_ge(dve_step, base - CT + m + 1)
                        i = v.scalar_tensor_tensor(y[:, m, :], u[:, m, k:k + T], w_dw[:, m, k:k + 1], y[:, m, :],
                                                   ALU.mult, ALU.add)
                    if k < TAPS - 1:
                        step(i)
                    else:
                        i.then_inc(y_ready, 1)
            take_mod(3, 2 * KT, 5 * KT).then_inc(mod_ready, 1)

            dve.wait_ge(y_ready, CT)
            dve.wait_ge(tile_done, N_LN + 1)
            v.tensor_scalar(rstd[:, :], ps[:, N_LN % BANKS, :], 1.0 / (CT * P), None, ALU.mult
                            ).then_inc(bank_free[N_LN % BANKS], 1)
            freed(dve, N_LN)
            for m in range(CT):
                v.tensor_tensor(y[:, m, :], y[:, m, :], rstd[:, :], ALU.subtract).then_inc(yc_ready, 1)
            freed(dve, N_LN + 1)
            step(v.reciprocal(rstd[:, :], std[:, :]))
            settled()
            dve.wait_ge(yc_ready, CT)
            for m in range(CT):
                v.tensor_tensor(y[:, m, :], y[:, m, :], rstd[:, :], ALU.mult).then_inc(yn_ready, 1)

            for d in range(KT):
                n = N_PROJ + 2 * d
                if d == 0:
                    for q in range(4):
                        freed(dve, N_GATE + 2 * KT - 4 + q)
                dve.wait_ge(tile_done, n + 2)
                v.tensor_tensor(gates[:, d, :], ps[:, n % BANKS, :], gates[:, d, :], ALU.mult
                                ).then_inc(bank_free[n % BANKS], 1)
                v.tensor_tensor(gates[:, KT + d, :], ps[:, (n + 1) % BANKS, :], gates[:, KT + d, :], ALU.mult
                                ).then_inc(bank_free[(n + 1) % BANKS], 1)
                freed(dve, n)
                freed(dve, n + 1)
                v.tensor_tensor(gates[:, d, :], gates[:, d, :], gates[:, KT + d, :], ALU.add).then_inc(merged, 1)

            dve.wait_ge(mod_ready, 2)
            for d in range(KT):
                n = N_WOUT + d
                dve.wait_ge(tile_done, n + 1)
                v.scalar_tensor_tensor(hT[:, d, :], ps[:, n % BANKS, :], mod[:, 2 * KT + d:2 * KT + d + 1], hT[:, d, :],
                                       ALU.mult, ALU.add).then_inc(bank_free[n % BANKS], 1)
            for k in range(4, KT):
                freed(dve, N_WOUT + k)
            scale_rows(1)
            v.scalar_tensor_tensor(coef[:, 1, :], mod[:, 4 * KT:5 * KT], 1.0, g2, ALU.add, ALU.mult
                                   ).then_inc(mod_ready, 1)

            base = count[0]
            per = [0]

            def hstep(ins, h):
                per[0] += 1
                ins.then_inc(dve_step, 1)

            def hsettled(h, e, k):
                dve.wait_ge(dve_step, h * k + base + per[0])
                v.sem_inc(dve_turn, 1)

            STEPS = 67
            with dve.Fori(0, PH // 2) as h2:
                h = h2 * 2
                per[0] = 0
                for e in range(2):
                    start = per[0]
                    dve.wait_ge(sc_ready, h + e + 2)
                    v.sem_inc(dve_turn, 1)
                    for b in range(TB):
                        for half in range(2):
                            hstep(v.max(vals[:, b, half, 0:8], sc[:, e, 2 * b + half, :]), h)
                    hsettled(h, e, STEPS)
                    for b in range(TB):
                        for half in range(2):
                            hstep(v.match_replace(out=sc2[:, 2 * b + half, :], in_to_replace=vals[:, b, half, 0:8],
                                                  in_values=sc[:, e, 2 * b + half, :], imm_value=NEG), h)
                            hstep(v.max_index(out=vidx[:, b, half, 0:8], in_max=vals[:, b, half, 0:8],
                                              in_values=sc[:, e, 2 * b + half, :]), h)
                    hsettled(h, e, STEPS)
                    for b in range(TB):
                        for half in range(2):
                            hstep(v.max(vals[:, b, half, 8:16], sc2[:, 2 * b + half, :]), h)
                    hsettled(h, e, STEPS)
                    for b in range(TB):
                        for half in range(2):
                            i = v.max_index(out=vidx[:, b, half, 8:16], in_max=vals[:, b, half, 8:16],
                                            in_values=sc2[:, 2 * b + half, :])
                            hstep(i, h)
                    for b in range(TB):
                        hstep(v.tensor_tensor(cand[:, b, :].rearrange("p (i j) -> p i j", i=TOPK),
                                              vals[:, b, 0, :].unsqueeze(2).broadcast_to([P, TOPK, TOPK]),
                                              vals[:, b, 1, :].unsqueeze(1).broadcast_to([P, TOPK, TOPK]), ALU.add), h)
                    hsettled(h, e, STEPS)
                    dve.wait_ge(sel_free, h + e + 1)
                    v.tensor_copy(vidf[e], vidx).then_inc(sc_free, 1)
                    for b in range(TB):
                        hstep(v.max(best[:, b, 0:8], cand[:, b, :]), h)
                    hsettled(h, e, STEPS)
                    for b in range(TB):
                        hstep(v.match_replace(out=cand2[:, b, :], in_to_replace=best[:, b, 0:8],
                                              in_values=cand[:, b, :], imm_value=NEG), h)
                        hstep(v.max_index(out=pos[:, b, 0:8], in_max=best[:, b, 0:8], in_values=cand[:, b, :]), h)
                    hsettled(h, e, STEPS)
                    for b in range(TB):
                        hstep(v.max(best[:, b, 8:16], cand2[:, b, :]), h)
                    hsettled(h, e, STEPS)
                    for b in range(TB):
                        hstep(v.max_index(out=pos[:, b, 8:16], in_max=best[:, b, 8:16], in_values=cand2[:, b, :]), h)
                    hstep(v.tensor_copy(bests[:, :, bass.ds(h + e, 1), :].rearrange("p b a k -> p b (a k)"),
                                        best[:, :, :]), h)
                    hsettled(h, e, STEPS)
                    hstep(v.tensor_scalar(posa[:, 0, :, :], pos[:, :, :], 4, None, ALU.logical_shift_right), h)
                    hstep(v.tensor_scalar(posa[:, 1, :, :], pos[:, :, :], 15, None, ALU.bitwise_and), h)
                    hsettled(h, e, STEPS)
                    v.tensor_copy(posf[e], posa).then_inc(pos_ready, 1)
                assert per[0] == 2 * STEPS, per
            count[0] = base + PH * STEPS

            dve.wait_ge(pos_ready, PH)
            v.tensor_tensor(gw, bests, bests[:, :, :, 0:1].broadcast_to([P, TB, PH, TOPK]), ALU.subtract
                            ).then_inc(sm_in, 1)
            take_mod(4, 5 * KT, 6 * KT).then_inc(mod_ready, 1)
            dve.wait_ge(mod_ready, 4)
            for k in range(KT):
                i = v.tensor_scalar(diag[:, k, :], ident[:, :], mod[:, 5 * KT + k:5 * KT + k + 1], None, ALU.mult)
            i.then_inc(mod_ready, 1)
            dve.wait_ge(sm_exp, 1)
            gv = gw.rearrange("p b h k -> p (b h) k")
            step(v.tensor_reduce(gsum[:, :], gv, axis=AX.X, op=ALU.add))
            settled()
            step(v.reciprocal(gsum[:, :], gsum[:, :]))
            settled()
            dve.wait_ge(sel_free, PH + 2)
            v.tensor_tensor(gv, gv, gsum[:, :].unsqueeze(2).broadcast_to([P, TB * PH, TOPK]), ALU.mult
                            ).then_inc(list_in, 1)
            v.scalar_tensor_tensor(eidx[:, :], isel[:, 0, :, :].rearrange("p h k -> p (h k)"), float(NK),
                                   jsel[:, 0, :, :].rearrange("p h k -> p (h k)"), ALU.mult, ALU.add
                                   ).then_inc(idx_ready, 1)

            for q in range(3):
                freed(dve, N_LIST + q)
            with dve.Fori(0, PIECES * 4) as it:
                for c in range(4):
                    dve.wait_ge(oh_used, it * 4 + c + 1)
                    for t in range(4):
                        tok = it * 16 + 4 * c + t
                        v.tensor_scalar(ohj[:, 4 * c + t, :], iotan[:, :], lists[:, 1, bass.ds(tok, 1)], None,
                                        ALU.is_equal)
                        i = v.tensor_scalar(ohi[:, 4 * c + t, :], iotan[:, :], lists[:, 0, bass.ds(tok, 1)],
                                            lists[:, 2, bass.ds(tok, 1)], ALU.is_equal, ALU.mult)
                    i.then_inc(oh_ready, 1)

            def rest_u(n, slot, a, first):
                dve.wait_ge(uhi_ready, n + 1)
                v.tensor_tensor(Us[:, a, 1, :], uraw[:, slot, a, :], Us[:, a, 0, :].bitcast(f32), ALU.subtract
                                ).then_inc(ulo_ready, 1)

            def weigh(n, slot, a, g, first):
                dve.wait_ge(gel_ready, n + 1)
                dve.wait_ge(g_here[slot], (g + 1) * 16)
                ga = gel[:, a, :].rearrange("p (h t) -> p h t", h=PIECES)
                v.tensor_tensor(ga, ga, graw[:, slot, :, a, :], ALU.mult).then_inc(a_ready, 1)
                if not first:
                    dve.wait_ge(v_done, n - 1)
                dve.wait_ge(a_ready, n + 1)
                v.tensor_copy(As[:, a, 0, :], gel[:, a, :]).then_inc(ahi_ready, 1)
                dve.wait_ge(ahi_ready, n + 1)
                v.tensor_tensor(As[:, a, 1, :], gel[:, a, :], As[:, a, 0, :].bitcast(f32), ALU.subtract
                                ).then_inc(alo_ready, 1)
                dve.wait_ge(vhi_ready, n + 1)
                v.tensor_tensor(Vs[:, a, 1, :], vraw[:, slot, a, :], Vs[:, a, 0, :].bitcast(f32), ALU.subtract
                                ).then_inc(vlo_ready, 1)

            def dot(g, s):
                dve.wait_ge(row_here[s], (g + 1) * 16)
                v.tensor_tensor_reduce(out=row[:, s, :], in0=row[:, s, :], in1=n_tok, scale=1.0, scalar=0.0,
                                       op0=ALU.mult, op1=ALU.add, accum_out=dot1[:, s:s + 1]).then_inc(row_used, 1)

            def dots_out(g):
                dve.wait_ge(row_used, g * ROWBUF + ROWBUF)
                v.tensor_copy(dots[:, bass.ds(g * ROWBUF, ROWBUF)], dot1[:, :]).then_inc(dots_ready, 1)
                dve.wait_ge(dots_ready, g + 1)

            def add_row(g, s):
                dve.wait_ge(row_here[s], (g + 1) * 16)
                dve.wait_ge(row_used, g * ROWBUF + (s - 1))
                v.scalar_tensor_tensor(acc[:, s % 2, :], row[:, s, :],
                                       act_w[:, bass.ds(g * ROWBUF + (s - SLOTS), 1)],
                                       acc[:, s % 2, :], ALU.mult, ALU.add).then_inc(row_used, 1)

            for n in range(4):
                rest_u(n, n // 2, n % 2, n < 2)
                if n:
                    weigh(n - 1, (n - 1) // 2, (n - 1) % 2, 0, n <= 2)
            half_way = XT // 8
            with dve.Fori(1, half_way + 1) as g:
                for c in range(4):
                    rest_u(g * 4 + c, c // 2, c % 2, False)
                    dot(g - 1, 2 * c)
                    m = (c - 1) % 4
                    weigh(g * 4 + (c - 1), m // 2, m % 2, g - 1 if c == 0 else g, False)
                    dot(g - 1, 2 * c + 1)
                dots_out(g - 1)
            step(v.memset(acc[:, 0, :], 0.0))
            step(v.memset(acc[:, 1, :], 0.0))
            dve.wait_ge(gelu_ready, 1)
            step(v.tensor_tensor(act_w[:, :], act_w[:, :], gw[:, 0, :, :].rearrange("p h k -> p (h k)"), ALU.mult))
            settled()
            with dve.Fori(half_way + 1, XT // 4) as g:
                for c in range(4):
                    rest_u(g * 4 + c, c // 2, c % 2, False)
                    add_row(g - 1, 2 * c)
                    m = (c - 1) % 4
                    weigh(g * 4 + (c - 1), m // 2, m % 2, g - 1 if c == 0 else g, False)
                    add_row(g - 1, 2 * c + 1)
            weigh(XT - 1, 1, 1, XT // 4 - 1, False)
            for s in range(ROWBUF):
                add_row(XT // 4 - 1, s)
            dve.wait_ge(row_used, 2 * SLOTS)
            step(v.tensor_tensor(acc[:, 0, :], acc[:, 0, :], acc[:, 1, :], ALU.add))
            settled()

            for b in range(TB):
                if b == 1:
                    dve.wait_ge(v_done, XT)
                src = acc[:, 0, :] if b == 0 else ps[:, 2 * b - 2:2 * b, :].rearrange("p h d -> p (h d)")
                if b >= 2:
                    dve.wait_ge(out_done[b % 2], 16 * (b // 2))
                step(v.tensor_tensor(yout[:, b % 2, :], src, g2row, ALU.mult))
                settled()
                v.tensor_tensor(yout[:, b % 2, :], yout[:, b % 2, :], h_tok[:, b, :], ALU.add).then_inc(y_sum, 1)
                dve.wait_ge(y_std, b + 1)
                step(v.reciprocal(srstd[:, b:b + 1], sstd[:, b:b + 1]))
                settled()
                v.scalar_tensor_tensor(yout[:, b % 2, :], yout[:, b % 2, :], srstd[:, b:b + 1], gfin, ALU.mult, ALU.mult
                                       ).then_inc(y_out, 1)


def slope_bias():
    slopes = (2.0 ** (-8.0 * np.arange(1, HEADS + 1) / HEADS)).astype(np.float32)
    q = np.arange(P)[:, None] + P
    k = np.arange(KEYS)[None, :]
    chunk = k // HD - q // HD
    seen = (chunk == 0) | (chunk == -1)
    dist = np.abs(q - k).astype(np.float32)
    order = [m + PAIRS * e for m in range(PAIRS) for e in range(2)]
    return np.stack([np.where(seen, -slopes[h] * dist, np.float32(-1e30)) for h in order], 1).astype(np.float32)


def tiles(w):
    n = w.shape[1] // P
    return w.reshape(-1, P, n, P).transpose(2, 1, 0, 3).reshape(n, P, -1)


def kernel(x, c, w_ada, b_ada, g_norm1, w_in, w_dw, b_dw, ln_g, ln_b, w_conv_out, w_attn_out, attn_sinks, w_out,
           g_norm2, w_pq, sub_keys, peer_u, peer_v, g_final):
    import concourse.bacc as _bacc
    from concourse import mybir as _mybir
    from concourse.bass_utils import run_bass_kernel_spmd as _run

    A = np.asarray
    w_in = A(w_in)[0]
    pair = [m + PAIRS * e for m in range(PAIRS) for e in range(2)]
    w_q = w_in[:, 1024:1536].reshape(D, HEADS, HD)[:, pair].reshape(D, -1)
    w_ao = A(w_attn_out)[0].reshape(HEADS, HD, D)[pair].reshape(-1, D)
    conv = tiles(w_in[:, 0:1024])[[0, 4, 1, 5, 2, 6, 3, 7]]
    ada = tiles(A(w_ada)[0])
    gate = tiles(w_in[:, 1792:3840])
    stream = np.concatenate([ada[0:16], conv, ada[16:24], gate[0:8], ada[24:32], gate[8:16], ada[32:40],
                             tiles(np.concatenate([A(w_conv_out)[0], w_ao])), tiles(A(w_out)[0]),
                             tiles(A(w_pq)[0]), ada[40:48]])
    stream = np.ascontiguousarray(stream.reshape(ROUNDS * 4, 2, P, -1).transpose(0, 2, 1, 3).reshape(ROUNDS * 4, P, -1))
    wqkv = tiles(np.concatenate([w_q, w_in[:, 1536:1792]], 1)).transpose(1, 0, 2).reshape(P, -1)
    col = lambda a: A(a).reshape(-1, P).T
    cols = np.concatenate([col(b_ada), col(g_norm1), col(g_norm2), col(b_dw), col(ln_g), col(ln_b),
                           A(w_dw)[0].T.reshape(CT, P, TAPS).transpose(1, 0, 2).reshape(P, -1), col(c)], 1)
    rows = np.broadcast_to(np.concatenate([A(attn_sinks)[0][pair], A(g_final)])[None], (P, HEADS + D))
    arrays = {
        "stream": stream, "wqkv": wqkv,
        "skT": A(sub_keys)[0].reshape(2 * PH, NK, P).transpose(2, 0, 1),
        "xT": A(x)[0].T.reshape(KT, P, T).transpose(1, 0, 2),
        "cols": cols, "rows": rows, "biasd": slope_bias(), "identd": np.eye(P, dtype=np.float32),
        "puT": tiles(A(peer_u)[0].T).reshape(XT // 2, 2, P, D).transpose(0, 2, 1, 3).reshape(XT // 2, P, -1),
        "pu": A(peer_u)[0], "pv": A(peer_v)[0],
    }
    arrays = {k: np.ascontiguousarray(a) for k, a in arrays.items()}
    nc = _bacc.Bacc("TRN2", target_bir_lowering=False, num_devices=1)
    aps = [nc.dram_tensor(k, a.shape, _mybir.dt.from_np(a.dtype), kind="ExternalInput").ap() for k, a in arrays.items()]
    out = nc.dram_tensor("out", (T, D), _mybir.dt.float32, kind="ExternalOutput").ap()
    gmat = nc.dram_tensor("gmat", (PIECES, P, NK * HT), _mybir.dt.float32, kind="Internal").ap()
    build(nc, *aps, gmat, out)
    r = _run(nc, [arrays], core_ids=[0])
    return r.results[0]["out"].reshape(1, T, D)
```

```python
import numpy as np
import concourse.bass as bass
from concourse import mybir
from contextlib import ExitStack

P = 128
D = 1024
T = 512
KT = D // P
TB = T // P
CT = 4
TAPS = 31
TAPS_BEFORE = 11
HEADS = 8
HD = 64
PAIRS = HEADS // 2
KEYS = 256
PH = 8
NK = 128
TOPK = 16
SLOTS = PH * TOPK
ROWBUF = 8
EPS = 1e-6

DB = TB - 1
DT = DB * P
XT = NK
HT = 32
PIECES = DT // HT
PRING = 3
EARLY = XT // 8
BODY = 16
LATE = BODY - BODY // 8
TURNS = XT // BODY

R_CONV, R_GATE, R_PROJ, R_WOUT, R_PQ, ROUNDS = 0, 1, 3, 4, 5, 7
MODS = 6
CAND = 65

N_RMS1 = 0
N_CONV = 1
N_QKV = N_CONV + 2 * CT
N_LN = N_QKV + 6
N_PROJ = N_LN + 2
N_WOUT = N_PROJ + 2 * KT - 4
N_RMS2 = N_WOUT + KT
N_PQ = N_RMS2 + 1
N_LIST = N_PQ + 2 * PH
BANKS = 4


def build(nc, stream, wada, wqkv, skT, xT, cols, rows, biasd, identd, puT, pu, pv, gmat, hsave, out):
    f32, f32r, i32, u32 = mybir.dt.float32, mybir.dt.float32r, mybir.dt.int32, mybir.dt.uint32
    ALU, ACT, AX = mybir.AluOpType, mybir.ActivationFunctionType, mybir.AxisListType
    NEG = -3.0e38

    with ExitStack() as ctx:
        def sb(name, shape, dt=f32):
            return ctx.enter_context(nc.sbuf_tensor(name, shape, dt))

        def sem(name):
            return ctx.enter_context(nc.semaphore(name))

        big = sb("big", [P, 4 * D * 4])
        wring = big[:, 0:8 * D].rearrange("p (s j k c) -> p s j k c", s=4, j=2, k=KT)
        hT = big[:, 8 * D:12 * D].rearrange("p (k t) -> p k t", k=KT)
        nT = big[:, 12 * D:16 * D].rearrange("p (k t) -> p k t", k=KT)
        place = ExitStack()
        mparts = place.enter_context(nc.sbuf_tensor("mparts", [P, 2, KT, T], f32r))
        place.close()
        mid = sb("mid", [P, 6 * D])
        qkvw = mid[:, :].rearrange("p (j k c) -> p j k c", j=6, k=KT)
        low = sb("low", [P, 4 * D])
        skw = low[:, 2 * D:4 * D].rearrange("p (h n) -> p h n", n=NK)
        bias = low[:, 0:2 * D].rearrange("p (h k) -> p h k", k=KEYS)
        aring = low[:, :].rearrange("p (s c) -> p s c", s=4)
        colv = sb("colv", [P, 208])
        rowv = sb("rowv", [P, HEADS + D])
        ident = sb("ident", [P, P])
        ones = sb("ones", [P, P])
        eps = sb("eps", [P, 1])
        cond = sb("cond", [P, KT])
        mod = sb("mod", [P, 6 * KT])
        coef = sb("coef", [P, 2, KT])
        stats = sb("stats", [P, 2 * T])
        std, rstd = stats[:, 0:T], stats[:, T:2 * T]
        nsink = sb("nsink", [P, HEADS])
        attnT = sb("attnT", [P, PAIRS, T])
        place = ExitStack()
        wparts = place.enter_context(nc.sbuf_tensor("wparts", [P, 2, 2, D], f32r))
        place.close()
        ptsb = sb("ptsb", [P, 2, 4, P])
        att = sb("att", [P, 8 * T])
        vtok = att[:, 5 * T:6 * T].rearrange("p (b d) -> p b d", b=TB)
        sq = att[:, 6 * T:8 * T].rearrange("p (a t) -> p a t", a=2)
        ssb = att[:, 0:2 * T].rearrange("p (r e k) -> p r e k", r=2, e=2)
        pexp = att[:, 2 * T:4 * T].rearrange("p (r e k) -> p r e k", r=2, e=2)
        nmx = sb("nmx", [P, 2, 2])
        mx = sb("mx", [P, 2, 2])
        rs = sb("rs", [P, 2, 2])
        es = sb("es", [P, 2, 2])
        den = sb("den", [P, 2, 2])
        rden = sb("rden", [P, 2, 2])
        dot1 = sb("dot1", [P, ROWBUF])
        dots = sb("dots", [P, SLOTS])
        act_w = sb("act_w", [P, SLOTS])
        islot = sb("islot", [P, ROWBUF], i32)
        eidx = sb("eidx", [P, SLOTS], i32)
        gsum = sb("gsum", [P, TB * PH])
        iotan = sb("iotan", [P, NK])
        zeros = sb("zeros", [P, P])
        ssum = sb("ssum", [P, TB])
        sstd = sb("sstd", [P, TB])
        srstd = sb("srstd", [P, TB])

        front = ExitStack()
        gates = front.enter_context(nc.sbuf_tensor("gates", [P, 2 * KT, T], f32))
        PADT = T + TAPS - 1
        WORK = CT * PADT + CT * T + 2 * T + PAIRS * T + T
        W = front.enter_context(nc.sbuf_tensor("work", [P, WORK], f32))
        u = W[:, 0:CT * PADT].rearrange("p (m t) -> p m t", m=CT)
        o0 = CT * PADT
        y = W[:, o0:o0 + CT * T].rearrange("p (m t) -> p m t", m=CT)
        o0 += CT * T
        sg = W[:, o0:o0 + 2 * T].rearrange("p (m t) -> p m t", m=2)
        o0 += 2 * T
        qT = W[:, o0:o0 + PAIRS * T].rearrange("p (m t) -> p m t", m=PAIRS)
        o0 += PAIRS * T
        kT = W[:, o0:o0 + T]
        front.close()
        macc = gates[:, 2 * KT - 2 * MODS:2 * KT, :].rearrange("p (q a) t -> p q (a t)", q=MODS)
        xs = sb("xs", [P, 2, KT, DT], f32r)
        As = sb("As", [P, 2, 2, DT], f32r)
        Us = sb("Us", [P, 2, 2, D], f32r)
        Vs = sb("Vs", [P, 2, 2, D], f32r)

        b_ada, g1, g2 = colv[:, 0:48], colv[:, 48:56], colv[:, 56:64]
        b_dw, ln_g, ln_b = colv[:, 64:68], colv[:, 68:72], colv[:, 72:76]
        w_dw = colv[:, 76:76 + CT * TAPS].rearrange("p (m k) -> p m k", m=CT)
        ccol = colv[:, 200:208]
        gfin = rowv[:, HEADS:HEADS + D]

        Q = mid[:, :]
        qh = Q[:, 0:4 * T].rearrange("p (e s t) -> p e s t", e=2, s=2)
        sc = Q[:, 4 * T:4 * T + 2 * 8 * NK].rearrange("p (e r n) -> p e r n", e=2, r=8)
        o1 = 4 * T + 2 * 8 * NK
        sc2 = Q[:, o1:o1 + 8 * NK].rearrange("p (r n) -> p r n", r=8)
        o1 += 8 * NK
        cand, cand2 = (Q[:, o1 + e * 512:o1 + e * 512 + TB * CAND].rearrange("p (b n) -> p b n", b=TB) for e in range(2))
        hot = low[:, 0:2 * D].rearrange("p (s b k a) -> p s b k a", s=2, b=TB, k=TOPK)
        A4 = attnT[:, :, :].rearrange("p m (b h k) -> p m b h k", h=PH, k=TOPK)
        bests, gw, isel, jsel = (A4[:, q] for q in range(4))
        eight = lambda o: att[:, o:o + TB * 2 * TOPK]
        vals, vidx = (eight(o).rearrange("p (b s k) -> p b s k", b=TB, s=2) for o in (0, 128))
        vidf = [eight(o).rearrange("p (b s k) -> p b s k", b=TB, s=2) for o in (256, 384)]
        posa = eight(512).rearrange("p (s b k) -> p s b k", b=TB, s=2).bitcast(u32)
        best, pos, seg, low4, sh, mask, c15 = (
            att[:, 768 + q * 64:768 + (q + 1) * 64].rearrange("p (b k) -> p b k", b=TB) for q in range(7))
        vidx, pos, seg, low4, sh, mask, c15 = (a.bitcast(u32) for a in (vidx, pos, seg, low4, sh, mask, c15))
        diag = sq[:, :, :].rearrange("p a (q c) -> p (a q) c", c=P)

        h_tok = mid[:, 0:4 * D].rearrange("p (b d) -> p b d", b=TB)
        n_tok = ptsb[:, :, :, :].rearrange("p a b c -> p (a b c)")
        g2row = stats[:, :]
        early = mid[:, 0:EARLY * DT].rearrange("p (n t) -> p n t", n=EARLY)

        piece = big[:, 4 * D:16 * D].rearrange("p (a i t) -> p a i t", a=PRING, i=NK)
        ohj = low[:, 0:2 * D].rearrange("p (s j) -> p s j", j=NK)
        ohi = low[:, 2 * D:4 * D].rearrange("p (s j) -> p s j", j=NK)
        ohj_side = big[:, 2 * D:2 * D + 3 * 4 * NK].rearrange("p (s t j) -> p s t j", s=3, t=4)
        lists = att[:, 0:3 * DT].rearrange("p (q t) -> p q t", q=3)

        uraw = big[:, 0:2 * D].rearrange("p (s f) -> p s f", s=2)
        vraw = big[:, 4 * D:8 * D].rearrange("p (s a f) -> p s a f", s=2, a=2)
        row = big[:, 8 * D:16 * D].rearrange("p (s f) -> p s f", f=D)
        acc = low[:, 0:2 * D].rearrange("p (a d) -> p a d", a=2)
        yout = row[:, 1:1 + TB, :]
        graw = att[:, 0:8 * DT].rearrange("p (s h a t) -> p s h a t", s=2, h=PIECES, a=4)
        gel = att[:, 8 * DT:10 * DT].rearrange("p (s t) -> p s t", s=2)

        ps = ctx.enter_context(nc.psum_tensor("ps", [P, 8, 512], f32))
        PT_B, O_B = ps[:, 6, :], ps[:, 7, :]
        MOD = ps[:, 7, 0:MODS * KT]
        MOD2 = ps[:, 3, KEYS:KEYS + MODS * KT]

        small_here = sem("small_here")
        x_here = sem("x_here")
        qkvw_here = sem("qkvw_here")
        late_here = sem("late_here")
        out_done = sem("out_done")
        w_here = [sem(f"w_here{s}") for s in range(4)]
        pair_begun = sem("pair_begun")
        ada_here = [sem(f"ada_here{e}") for e in range(4)]
        ada_used, macc_ready = sem("ada_used"), sem("macc_ready")
        consts = sem("consts")
        cond_ready = sem("cond_ready")
        tile_done = sem("tile_done")
        bank_free = [sem(f"bank_free{b}") for b in range(BANKS)]
        mod_done = sem("mod_done")
        mod_ready = sem("mod_ready")
        sq_ready, sq_used = sem("sq_ready"), sem("sq_used")
        scaled = sem("scaled")
        n_ready = sem("n_ready")
        gate_done, gate_taken = sem("gate_done"), sem("gate_taken")
        gates_ready = sem("gates_ready")
        s_done, s_biased = sem("s_done"), sem("s_biased")
        nmx_ready, exp_done, p_ready = sem("nmx_ready"), sem("exp_done"), sem("p_ready")
        pt_done, pt_ready = sem("pt_done"), sem("pt_ready")
        o_done, o_ready = sem("o_done"), sem("o_ready")
        dve_step = sem("dve_step")
        dve_turn = sem("dve_turn")
        y_ready, yc_ready, yn_ready, silu_ready = sem("y_ready"), sem("yc_ready"), sem("yn_ready"), sem("silu_ready")
        wout_hi, wout_lo = sem("wout_hi"), sem("wout_lo")
        merged_hi, merged_lo = sem("merged_hi"), sem("merged_lo")
        merged = sem("merged")
        attn_projected, attn_merged = sem("attn_projected"), sem("attn_merged")
        sc_done, sc_ready, sc_free = sem("sc_done"), sem("sc_ready"), sem("sc_free")
        pos_ready, sel_free = sem("pos_ready"), sem("sel_free")
        pool_step = sem("pool_step")
        sm_in, sm_exp = sem("sm_in"), sem("sm_exp")
        list_in = sem("list_in")
        xhi_ready, xlo_ready = sem("xhi_ready"), sem("xlo_ready")
        diff_ready, squared, ohj_ready = sem("diff_ready"), sem("squared"), sem("ohj_ready")
        oh_ready, oh_used, g_taken = sem("oh_ready"), sem("oh_used"), sem("g_taken")
        piece_out = [sem(f"piece_out{k}") for k in range(PRING)]
        side_done, side_free = sem("side_done"), sem("side_free")
        h_saved, h_here = [sem(f"h_saved{e}") for e in range(2)], sem("h_here")
        u_here, v_here, g_here = ([sem(f"{w}_here{e}") for e in range(2)] for w in "uvg")
        ulo_early = sem("ulo_early")
        uhi_ready, ulo_ready, vhi_ready, vlo_ready = (sem(f"{w}_ready") for w in ("uhi", "ulo", "vhi", "vlo"))
        u_done, v_done = sem("u_done"), sem("v_done")
        gel_ready, a_ready, ahi_ready, alo_ready = (sem(f"{w}_ready") for w in ("gel", "a", "ahi", "alo"))
        idx_ready = sem("idx_ready")
        slot_copied, pool_turn = sem("slot_copied"), sem("pool_turn")
        row_here = [sem(f"row_here{b}") for b in range(ROWBUF)]
        row_used = sem("row_used")
        dots_ready, gelu_ready = sem("dots_ready"), sem("gelu_ready")
        y_sum, y_sq, y_std, y_out = sem("y_sum"), sem("y_sq"), sem("y_std"), sem("y_out")

        def freed(eng, n):
            eng.wait_ge(bank_free[n % BANKS], n // BANKS + 1)

        block = ctx.enter_context(nc.Block())

        @block.sync
        def _(sp):
            sp.dma_start(colv[:, :], cols).then_inc(small_here, 16)

            def load_round(r, wait):
                for s in range(4):
                    if wait:
                        sp.wait_ge(pair_begun, r * 4 + s - 2)
                    sp.dma_start(wring[:, s, :, :, :].rearrange("p a b c -> p (a b c)"),
                                 stream[bass.ds(r * 4 + s, 1), :, :].rearrange("a p f -> (a p) f")
                                 ).then_inc(w_here[s], 16)
            def load_ada(g, wait):
                for e in range(4):
                    if wait:
                        sp.wait_ge(ada_used, g * 4 + e - 3)
                    sp.dma_start(aring[:, e, :], wada[bass.ds(g * 4 + e, 1), :, :].rearrange("a p f -> (a p) f")
                                 ).then_inc(ada_here[e], 16)
            load_ada(0, False)
            sp.dma_start(hT, xT).then_inc(x_here, 16)
            with sp.Fori(1, 2 * KT // 4) as g:
                load_ada(g, True)
            load_round(0, False)
            sp.dma_start(mid[:, :], wqkv).then_inc(qkvw_here, 16)
            with sp.Fori(2 * KT // 4, MODS * KT // 4) as g:
                load_ada(g, True)
            sp.dma_start(ident[:, :], identd).then_inc(late_here, 16)
            sp.dma_start(rowv[:, :], rows).then_inc(late_here, 16)
            sp.wait_ge(ada_used, MODS * KT)
            sp.dma_start(bias, biasd).then_inc(late_here, 16)
            sp.dma_start(skw, skT).then_inc(late_here, 16)
            with sp.Fori(1, ROUNDS) as r:
                load_round(r, True)

            sp.wait_ge(tile_done, N_LIST)

            def load_u(n, e):
                sp.dma_start(uraw[:, e, :], puT[bass.ds(n, 1), :, :].rearrange("a p f -> (a p) f")
                             ).then_inc(u_here[e], 16)
            for n in range(2):
                load_u(n, n)

            def piece_to_dram(r, k):
                sp.wait_ge(g_taken, r * 24 + 8 * (k + 1) + 4)
                sp.dma_start(gmat[bass.ds(r * PRING + k, 1), :, :].rearrange("a p f -> (a p) f"),
                             piece[:, k, :, :].rearrange("p i t -> p (i t)")).then_inc(piece_out[k], 16)
            with sp.Fori(0, PIECES // PRING) as r:
                for i, k in enumerate((None, 0, 1, 2)):
                    sp.wait_ge(ulo_early, r * 4 + i + 1)
                    load_u(r * 4 + i + 2, i % 2)
                    if k is not None:
                        piece_to_dram(r, k)

            def load_v(g, e):
                sp.wait_ge(vlo_ready, g * BODY + 2 * e + 2)
                sp.dma_start(vraw[:, e % 2, :, :],
                             pv[bass.ds((g * BODY + 2 * e) * P, 2 * P), :].rearrange("(a p) f -> p a f", p=P)
                             ).then_inc(v_here[e % 2], 16)

            def load_g(g, q):
                sp.wait_ge(a_ready, g * BODY + 4 * q + 4)
                sp.dma_start(graw[:, q % 2, :, :, :].rearrange("p h a t -> p h (a t)"),
                             gmat[:, :, bass.ds((g * BODY + 4 * q) * HT, 4 * HT)].rearrange("h p f -> p h f")
                             ).then_inc(g_here[q % 2], 16)

            def load_turn(g, last=False):
                i = 0
                for e in range(BODY // 2):
                    if e % 2 == 0:
                        load_g(g, e // 2)
                    load_v(g, e)
                    for _ in range(1 if e % 4 == 3 else 2):
                        if not (last and i >= LATE - 2):
                            sp.wait_ge(ulo_ready, g * LATE + i + 1)
                            load_u(g * LATE + (EARLY + 2 + i), i % 2)
                        i += 1
            for k in range(PRING):
                sp.wait_ge(piece_out[k], 16 * (PIECES // PRING + 1))
            sp.wait_ge(ulo_early, EARLY + 1)
            with sp.Fori(0, TURNS - 1) as g:
                load_turn(g)
            for e in range(2):
                sp.wait_ge(h_saved[e], 16 * (TB + 1))
            sp.wait_ge(alo_ready, 8 * (-(-4 * D // DT)) + 3)
            sp.dma_start(h_tok, hsave.rearrange("p (b d) -> p b d", b=TB)).then_inc(h_here, 16)
            load_turn(TURNS - 1, True)
            for b in range(TB):
                sp.wait_ge(y_out, b + 1)
                sp.dma_start(out[b * P:(b + 1) * P, :], yout[:, b, :]).then_inc(out_done, 16)
            sp.wait_ge(out_done, 16 * TB)

        @block.gpsimd
        def _(pool):
            nc.gpsimd.memset(ones[:, :], 1.0).then_inc(consts, 1)
            nc.gpsimd.memset(eps[:, :], EPS).then_inc(consts, 1)
            nc.gpsimd.memset(u[:, :, 0:TAPS - 1], 0.0).then_inc(consts, 1)
            nc.gpsimd.iota(iotan[:, :], pattern=[[1, NK]], base=0, channel_multiplier=0,
                           allow_small_or_imprecise_dtypes=True).then_inc(consts, 1)

            for k in range(KT):
                pool.wait_ge(xhi_ready, k + 1)
                nc.gpsimd.tensor_tensor(xs[:, 1, k, :], nT[:, k, P:T], xs[:, 0, k, :].bitcast(f32), ALU.subtract
                                        ).then_inc(xlo_ready, 1)

            nc.gpsimd.memset(zeros[:, :], 0.0).then_inc(consts, 1)

            nc.gpsimd.sem_inc(sel_free, 1)
            STEPS = 9
            def select(h2, heads=2):
                for e in range(heads):
                    n = [e * STEPS]
                    h = h2 * 2 + e

                    def pstep(ins):
                        n[0] += 1
                        ins.then_inc(pool_step, 1)
                        pool.wait_ge(pool_step, h2 * (2 * STEPS) + n[0])
                        nc.gpsimd.sem_inc(pool_turn, 1)

                    pool.wait_ge(pos_ready, h + 1)
                    for half, dst in enumerate((isel, jsel)):
                        x = hot[:, half]
                        pstep(nc.gpsimd.tensor_tensor(x, x, vidf[e][:, :, half, :].unsqueeze(2)
                                                      .broadcast_to([P, TB, TOPK, TOPK]), ALU.mult))
                        for w in (8, 4, 2):
                            pstep(nc.gpsimd.tensor_tensor(x[:, :, :, 0:w], x[:, :, :, 0:w], x[:, :, :, w:2 * w],
                                                          ALU.add))
                        i = nc.gpsimd.tensor_tensor(dst[:, :, bass.ds(h, 1), :].rearrange("p b a k -> p b (a k)"),
                                                    x[:, :, :, 0], x[:, :, :, 1], ALU.add)
                        if half == 0:
                            pstep(i)
                        else:
                            i.then_inc(sel_free, 1)
            with pool.Fori(0, PH // 2 - 1) as h2:
                select(h2)
            select(PH // 2 - 1, 1)

            def rest_early(n, e):
                pool.wait_ge(uhi_ready, n + 1)
                nc.gpsimd.sem_inc(pool_turn, 1)
                nc.gpsimd.tensor_tensor(Us[:, e, 1, :], uraw[:, e, :], Us[:, e, 0, :].bitcast(f32), ALU.subtract
                                        ).then_inc(ulo_early, 1)
            def difference(it, i):
                pool.wait_ge(oh_used, it * 24 + i + 1)
                nc.gpsimd.sem_inc(pool_turn, 1)
                nc.gpsimd.tensor_tensor(ohj_side[:, i // 4 % 3], iotan[:, :].unsqueeze(1).broadcast_to([P, 4, NK]),
                                        lists[:, 1, bass.ds(it * 96 + 4 * i, 4)].unsqueeze(2).broadcast_to([P, 4, NK]),
                                        ALU.subtract).then_inc(diff_ready, 1)

            rest_early(0, 0)
            for q in range(3):
                freed(pool, N_LIST + q)
            with pool.Fori(0, PIECES // PRING) as it:
                for i in range(3, 24, 4):
                    difference(it, i)
                    j = {3: 1, 7: 2, 15: 3, 23: 4}.get(i)
                    if j is not None:
                        rest_early(it * 4 + j, j % 2)

            def fetch(table, k0, r0, wait):
                for s in range(ROWBUF):
                    if wait:
                        pool.wait_ge(row_used, k0 + (r0 - ROWBUF + s + 1))
                    nc.gpsimd.tensor_copy(islot[:, s:s + 1], eidx[:, bass.ds(k0 + s, 1)]).then_inc(slot_copied, 1)
                    pool.wait_ge(slot_copied, k0 + (r0 + s + 1))
                    nc.gpsimd.sem_inc(pool_turn, 1)
                    nc.gpsimd.indirect_dma_start(
                        out=row[:, s, :], out_offset=None, in_=table,
                        in_offset=bass.IndirectOffsetOnAxis(ap=islot[:, s:s + 1], axis=0)).then_inc(row_here[s], 16)
            pool.wait_ge(idx_ready, 1)
            for k in range(PRING):
                pool.wait_ge(piece_out[k], 16 * (PIECES // PRING + 1))
            fetch(pu, 0, 0, False)
            with pool.Fori(1, SLOTS // ROWBUF) as group:
                fetch(pu, group * ROWBUF, 0, True)
            with pool.Fori(0, SLOTS // ROWBUF) as group:
                fetch(pv, group * ROWBUF, SLOTS, True)

        @block.tensor
        def _(pe):
            def bank(n):
                if n >= BANKS:
                    pe.wait_ge(bank_free[n % BANKS], n // BANKS)
                return ps[:, n % BANKS, :]

            def column_sums(n, sq0, count):
                o = bank(n)
                for k in range(count):
                    pe.wait_ge(sq_ready, sq0 + k + 1)
                    mm = nc.tensor.matmul(o, ones[:, :], sq[:, (sq0 + k) % 2, :], start=(k == 0), stop=(k == count - 1))
                    mm.then_inc(sq_used if k < count - 1 else tile_done, 1)

            def modulation(q):
                pe.wait_ge(macc_ready, q + 1)
                for c in range(KT):
                    mm = nc.tensor.matmul((MOD if q < 2 else MOD2)[:, q * KT + c:q * KT + c + 1], macc[:, q, c * P:(c + 1) * P], ones[:, 0:1],
                                          start=True, stop=True)
                return mm

            def product(o, lhs, rhs, count=KT, begins=False, need=None):
                for k in range(count):
                    if need is not None:
                        pe.wait_ge(n_ready, need + k + 1)
                    mm = nc.tensor.matmul(o, lhs(k), rhs(k), start=(k == 0), stop=(k == count - 1))
                    if begins and k == 0:
                        mm.then_inc(pair_begun, 1)
                return mm

            pe.wait_ge(consts, 1)
            column_sums(N_RMS1, 0, KT)
            modulation(0)
            modulation(1).then_inc(mod_done, 1)

            for s in range(4):
                pe.wait_ge(w_here[s], (R_CONV + 1) * 16)
                for j in range(2):
                    mm = product(bank(N_CONV + 2 * s + j), lambda k: wring[:, s, j, k, :], lambda k: nT[:, k, :], begins=j == 0,
                                 need=0 if s == 0 and j == 0 else None)
                    mm.then_inc(tile_done, 1)

            pe.wait_ge(qkvw_here, 16)
            for j in range(5):
                mm = product(bank(N_QKV + j), lambda k: qkvw[:, j, k, :], lambda k: nT[:, k, :])
                mm.then_inc(tile_done, 1)
            o = bank(N_QKV + 5)
            for b in range(TB):
                mm = product(o[:, b * P:(b + 1) * P], lambda k: nT[:, k, b * P:(b + 1) * P], lambda k: qkvw[:, 5, k, :])
            mm.then_inc(tile_done, 1)

            pe.wait_ge(mod_ready, 1)
            for j in range(2, 6):
                freed(pe, N_QKV + j)
            pe.wait_ge(late_here, 64)

            def att_scores(a):
                b, m = divmod(a, PAIRS)
                if a >= 2:
                    pe.wait_ge(s_biased, a - 1)
                if a % 2 and a // 2 + 1 in range(2, MODS):
                    q = a // 2 + 1
                    mm = modulation(q)
                    if q == MODS - 1:
                        mm.then_inc(mod_done, 1)
                k0, c0 = (0, P) if b == 0 else ((b - 1) * P, 0)
                for e in range(2):
                    mm = nc.tensor.matmul(ps[:, 2 * (a % 2) + e, c0:KEYS], qT[e * HD:(e + 1) * HD, m, b * P:(b + 1) * P],
                                          kT[e * HD:(e + 1) * HD, k0:(b + 1) * P], start=True, stop=True)
                mm.then_inc(s_done, 1)

            def gate_tile(a):
                s, j = a % 8 // 2, a % 2
                if j == 0:
                    pe.wait_ge(w_here[s], (a // 8 + R_GATE + 1) * 16)
                if a >= 2:
                    pe.wait_ge(gate_taken, a - 1)
                mm = product(ps[:, 4 + a % 2, :], lambda k: wring[:, s, j, k, :], lambda k: nT[:, k, :], begins=j == 0)
                mm.then_inc(gate_done, 1)

            def att_out(a):
                b, m = divmod(a, PAIRS)
                tiles = (1,) if b == 0 else (0, 1)
                pe.wait_ge(p_ready, a + 1)
                if a >= 1:
                    pe.wait_ge(pt_ready, a)
                for e in range(2):
                    for c in tiles:
                        mm = nc.tensor.transpose(PT_B[:, (2 * e + c) * P:(2 * e + c + 1) * P],
                                                 pexp[:, a % 2, e, c * P:(c + 1) * P], ident[:, :])
                mm.then_inc(pt_done, 1)
                if a + 2 < TB * PAIRS:
                    att_scores(a + 2)
                if a + 1 < TB * PAIRS:
                    gate_tile(a + 1)
                pe.wait_ge(pt_ready, a + 1)
                if m == 0 and b >= 1:
                    pe.wait_ge(o_ready, b)
                for e in range(2):
                    for c in tiles:
                        mm = nc.tensor.matmul(O_B[e * HD:(e + 1) * HD, m * P:(m + 1) * P],
                                              vtok[:, b - 1 + c, e * HD:(e + 1) * HD], ptsb[:, a % 2, 2 * e + c, :],
                                              start=(c == tiles[0]), stop=(c == 1))
                if m == PAIRS - 1:
                    mm.then_inc(o_done, 1)

            att_scores(0)
            att_scores(1)
            gate_tile(0)
            for a in range(TB * PAIRS):
                att_out(a)

            pe.wait_ge(s_biased, TB * PAIRS)
            pe.wait_ge(mod_ready, 2)
            o = bank(N_LN)
            pe.wait_ge(y_ready, CT)
            mm = product(o, lambda k: ones[:, :], lambda k: y[:, k, :], CT)
            mm.then_inc(tile_done, 1)

            def attn_projection(d):
                if d == 0:
                    pe.wait_ge(gate_taken, 2 * KT)
                    pe.wait_ge(o_ready, TB)
                if d % 2 == 0:
                    pe.wait_ge(w_here[d // 2], (R_PROJ + 1) * 16)
                mm = product(ps[:, 4 + d, :], lambda k: wring[:, d // 2, d % 2, CT + k, :], lambda k: attnT[:, k, :], CT)
                mm.then_inc(attn_projected, 1)
            attn_projection(0)
            column_sums(N_LN + 1, KT, CT)
            for d in range(1, 4):
                attn_projection(d)

            pe.wait_ge(silu_ready, CT)
            for s in range(4):
                if s >= 2:
                    pe.wait_ge(w_here[s], (R_PROJ + 1) * 16)
                for j in range(2):
                    d = 2 * s + j
                    n = N_PROJ + (d if d < 4 else 2 * d - 4)
                    mm = product(bank(n), lambda k: wring[:, s, j, k, :], lambda k: y[:, k, :], CT, begins=j == 0)
                    mm.then_inc(tile_done, 1)
                    if d >= 4:
                        mm = product(bank(n + 1), lambda k: wring[:, s, j, CT + k, :], lambda k: attnT[:, k, :], CT)
                        mm.then_inc(tile_done, 1)

            for d in range(KT):
                pe.wait_ge(wout_lo, d + 1)
                o = bank(N_WOUT + d)
                for k in range(KT):
                    if d == 0:
                        pe.wait_ge(merged_lo, k + 1)
                    hi, lo = (wparts[:, d % 2, w, k * P:(k + 1) * P] for w in range(2))
                    for a, b in ((hi, 0), (hi, 1), (lo, 0)):
                        mm = nc.tensor.matmul(o, a, mparts[:, b, k, :], start=(k == 0 and a is hi and b == 0),
                                              stop=(k == KT - 1 and a is lo))
                        if d % 2 == 0 and k == 0 and a is hi and b == 0:
                            mm.then_inc(pair_begun, 1)
                mm.then_inc(tile_done, 1)

            column_sums(N_RMS2, KT + CT, KT)

            def transposed(i, src, b, half):
                pe.wait_ge(side_free, i - 1)
                for q in range(4):
                    mm = nc.tensor.transpose(ps[:, 6 + i % 2, q * P:(q + 1) * P],
                                             src[:, 4 * half + q, b * P:(b + 1) * P], ident[:, :])
                mm.then_inc(side_done, 1)

            for r in range(2):
                for s in range(4):
                    pe.wait_ge(w_here[s], (r + R_PQ + 1) * 16)
                    for j in range(2):
                        n0 = N_PQ + 2 * s + j
                        pe.wait_ge(bank_free[n0 % BANKS], r * 2 + n0 // BANKS)
                        mm = product(ps[:, n0 % BANKS, :], lambda k: wring[:, s, j, k, :], lambda k: nT[:, k, :],
                                     begins=j == 0, need=KT if r == s == j == 0 else None)
                        mm.then_inc(tile_done, 1)
                    if r == s == 0:
                        pe.wait_ge(mod_ready, 4)
                        for half in range(2):
                            for q in range(4):
                                mm = nc.tensor.matmul(ps[:, 6 + half, q * P:(q + 1) * P], ones[:, :],
                                                      diag[:, 4 * half + q, :], start=True, stop=True)
                            mm.then_inc(side_done, 1)
                    pe.wait_ge(bank_free[(N_PQ + 2 * s) % BANKS], r * 2 + (N_PQ + 2 * s) // BANKS + 1)
                    pe.wait_ge(bank_free[(N_PQ + 2 * s + 1) % BANKS], r * 2 + (N_PQ + 2 * s + 1) // BANKS + 1)
                    pe.wait_ge(sc_ready, r * 4 + s + 1)
                    for b in range(TB):
                        for half in range(2):
                            mm = nc.tensor.matmul(
                                ps[:, 4 + b // 2, ((b % 2) * 2 + half) * NK:((b % 2) * 2 + half + 1) * NK],
                                qh[:, s % 2, half, b * P:(b + 1) * P],
                                skw[:, bass.ds(r * 8 + 2 * s + half, 1), :].rearrange("p a n -> p (a n)"),
                                start=True, stop=True)
                    mm.then_inc(sc_done, 1)
                    w = r * 4 + s
                    transposed(2 + w, hT, w // 2, w % 2)
            for half in range(2):
                transposed(2 + 2 * TB + half, nT, 0, half)

            pe.wait_ge(list_in, 1)
            for q, src in enumerate((isel, jsel, gw)):
                o = bank(N_LIST + q)
                for b in range(DB):
                    mm = nc.tensor.transpose(o[:, b * P:(b + 1) * P],
                                             src[:, b + 1, :, :].rearrange("p h k -> p (h k)"), ident[:, :])
                mm.then_inc(tile_done, 1)

            for q in range(3):
                freed(pe, N_LIST + q)
            pe.wait_ge(side_free, 2 * TB + 4)
            nc.tensor.sem_inc(oh_used, 12)

            def hidden(n, e, early=False):
                if early:
                    pe.wait_ge(ulo_early, n + 1)
                else:
                    pe.wait_ge(ulo_ready, n - (EARLY - 1))
                pe.wait_ge(gel_ready, n + 1)
                for k in range(KT):
                    hi, lo = (Us[:, e, w, k * P:(k + 1) * P] for w in range(2))
                    for a, b in ((hi, 0), (hi, 1), (lo, 0)):
                        mm = nc.tensor.matmul(ps[:, 6 + e, 0:DT], a, xs[:, b, k, :],
                                              start=(k == 0 and a is hi and b == 0), stop=(k == KT - 1 and a is lo))
                mm.then_inc(u_done, 1)

            pe.wait_ge(xlo_ready, KT)
            with pe.Fori(0, PIECES // PRING) as it:
                for i in range(24):
                    c = i % 4
                    pe.wait_ge(oh_ready, it * 24 + i + 1)
                    if c == 3:
                        pe.wait_ge(ohj_ready, it * 6 + i // 4 + 1)
                    pe.wait_ge(g_taken, it * 24 + i + 1)
                    for t in range(4):
                        rows_j = ohj[:, 4 * c + t, :] if c < 3 else ohj_side[:, i // 4 % 3, t, :]
                        mm = nc.tensor.matmul(ps[:, c, t * P:(t + 1) * P], rows_j, ohi[:, 4 * c + t, :],
                                              start=True, stop=True)
                    mm.then_inc(oh_used, 1)
                    if i % 6 == 2:
                        hidden(it * 4 + i // 6, i // 6 % 2, True)

            def output(o, e, last=False):
                pe.wait_ge(alo_ready, o + (1 + 3))
                pe.wait_ge(vlo_ready, o + (1 + 4))
                for b in range(DB):
                    hi, lo = (As[:, e, w, b * P:(b + 1) * P] for w in range(2))
                    for a, w in ((hi, 0), (hi, 1), (lo, 0)):
                        for half in range(2):
                            mm = nc.tensor.matmul(ps[:, 2 * b + half, :], a, Vs[:, e, w, half * T:(half + 1) * T],
                                                  start=False, stop=(last and a is lo))
                    if last or b == DB - 1:
                        mm.then_inc(v_done, 1)

            def dense_turn(g, last=False):
                for d in range(BODY):
                    nxt = d + 1
                    if nxt % 8 != 7 and not (last and nxt == BODY):
                        i = nxt - nxt // 8
                        hidden(g * LATE + (EARLY + i), i % 2)
                    output(g * BODY + d, d % 2, last and d == BODY - 1)

            hidden(EARLY, 0, True)
            pe.wait_ge(g_taken, PIECES * 8 + 4)
            pe.wait_ge(consts, 5)
            for b in range(2 * DB):
                nc.tensor.matmul(ps[:, b, :], zeros[:, :], gfin[:, 0:T], start=True, stop=False)
            with pe.Fori(0, TURNS - 1) as g:
                dense_turn(g)
            dense_turn(TURNS - 1, True)

        @block.scalar
        def _(act):
            f = nc.scalar.activation
            act.wait_ge(small_here, 16)
            f(cond[:, :], ccol, ACT.Silu).then_inc(cond_ready, 1)

            def squares(src, n0, used, count, need):
                for k in range(count):
                    need(k)
                    if k >= 2:
                        act.wait_ge(sq_used, used + k - 1)
                    f(sq[:, (n0 + k) % 2, :], src(k), ACT.Square).then_inc(sq_ready, 1)

            def root(n, count):
                act.wait_ge(tile_done, n + 1)
                f(std, ps[:, n % BANKS, :], ACT.Sqrt, bias=eps[:, 0:1], scale=1.0 / count
                  ).then_inc(bank_free[n % BANKS], 1)

            def modulate(stage, shift0):
                for k in range(KT):
                    act.wait_ge(scaled, stage * KT + k + 1)
                    f(nT[:, k, :], nT[:, k, :], ACT.Identity, scale=coef[:, stage, k:k + 1],
                      bias=mod[:, shift0 + k:shift0 + k + 1]).then_inc(n_ready, 1)

            act.wait_ge(x_here, 16)
            squares(lambda k: hT[:, k, :], 0, 0, KT, lambda k: None)
            act.wait_ge(consts, 3)
            root(N_RMS1, D)
            act.wait_ge(mod_ready, 1)
            modulate(0, 0)

            for m in range(CT):
                n = N_CONV + 2 * m + 1
                act.wait_ge(tile_done, n + 1)
                if m >= 2:
                    freed(act, n - 5)
                f(sg[:, m % 2, :], ps[:, n % BANKS, :], ACT.Sigmoid).then_inc(bank_free[n % BANKS], 1)
            for j in range(6):
                n = N_QKV + j
                act.wait_ge(tile_done, n + 1)
                dst = (qT[:, j, :] if j < 4 else kT[:, :] if j == 4 else
                       vtok[:, :, :].rearrange("p b d -> p (b d)"))
                f(dst, ps[:, n % BANKS, :], ACT.Copy, scale=HD ** -0.5 if j < 4 else 1.0
                  ).then_inc(bank_free[n % BANKS], 1)

            def att_evac(a):
                b = a // PAIRS
                act.wait_ge(pt_done, a + 1)
                s0 = P if b == 0 else 0
                view = lambda t: t.rearrange("p (e k) -> p e k", e=2)[:, :, s0:KEYS]
                f(view(ptsb[:, a % 2, :, :].rearrange("p c q -> p (c q)")), view(PT_B), ACT.Copy).then_inc(pt_ready, 1)
                if a % PAIRS == PAIRS - 1:
                    act.wait_ge(o_done, b + 1)
                    f(attnT[:, :, b * P:(b + 1) * P], O_B.rearrange("p (m q) -> p m q", m=PAIRS), ACT.Copy
                      ).then_inc(o_ready, 1)
            def gate_evac(a):
                act.wait_ge(gate_done, a + 1)
                f(gates[:, a, :], ps[:, 4 + a % 2, :], ACT.Copy).then_inc(gate_taken, 1)
            for a in range(TB * PAIRS):
                c0 = P if a < PAIRS else 0
                act.wait_ge(nmx_ready, a + 1)
                if a >= 2:
                    act.wait_ge(pt_done, a - 1)
                for e in range(2):
                    f(pexp[:, a % 2, e, c0:KEYS], ssb[:, a % 2, e, c0:KEYS], ACT.Exp, bias=nmx[:, a % 2, e:e + 1],
                      accum_out=rs[:, a % 2, e:e + 1])
                f(es[:, a % 2, :], mx[:, a % 2, :], ACT.Exp).then_inc(exp_done, 1)
                if a >= 1:
                    att_evac(a - 1)
                    gate_evac(a - 1)
            att_evac(TB * PAIRS - 1)
            gate_evac(TB * PAIRS - 1)

            squares(lambda k: y[:, k, :], KT, KT - 1, CT, lambda k: act.wait_ge(yc_ready, k + 1))
            root(N_LN + 1, CT * P)
            for m in range(CT):
                act.wait_ge(yn_ready, m + 1)
                f(y[:, m, :], y[:, m, :], ACT.Silu, scale=ln_g[:, m:m + 1], bias=ln_b[:, m:m + 1]).then_inc(silu_ready, 1)
            act.wait_ge(gate_taken, TB * PAIRS)
            for j in (0, 2, 1, 3):
                f(gates[:, 4 * j:4 * j + 4, :], gates[:, 4 * j:4 * j + 4, :], ACT.Sigmoid).then_inc(gates_ready, 1)

            def wout_round(d):
                act.wait_ge(w_here[d // 2], (R_WOUT + 1) * 16)
                if d >= 2:
                    act.wait_ge(tile_done, N_WOUT + d - 1)
                f(wparts[:, d % 2, 0, :], wring[:, d // 2, d % 2, :, :].rearrange("p k c -> p (k c)"), ACT.Copy
                  ).then_inc(wout_hi, 1)
            wout_round(0)
            wout_round(1)
            for k in range(KT):
                act.wait_ge(merged, k + 1)
                f(mparts[:, 0, k, :], gates[:, k, :], ACT.Copy).then_inc(merged_hi, 1)
            for d in range(2, KT):
                wout_round(d)

            squares(lambda k: hT[:, k, :], KT + CT, KT + CT - 2, KT, lambda k: freed(act, N_WOUT + k))
            root(N_RMS2, D)
            act.wait_ge(mod_ready, 3)
            modulate(1, 3 * KT)

            for k in range(KT):
                act.wait_ge(n_ready, KT + k + 1)
                f(xs[:, 0, k, :], nT[:, k, P:T], ACT.Copy).then_inc(xhi_ready, 1)

            for half in range(2):
                act.wait_ge(side_done, half + 1)
                f(g2row[:, half * T:(half + 1) * T], ps[:, 6 + half, :], ACT.Copy).then_inc(side_free, 1)

            nc.scalar.sem_inc(sc_ready, 1)
            nc.scalar.sem_inc(sc_free, 2)
            for e in range(2):
                nc.scalar.sem_inc(h_saved[e], 16)
            with act.Fori(0, PH // 2) as h2:
                h = h2 * 2
                for e in range(2):
                    for half in range(2):
                        n0 = N_PQ + 2 * e + half
                        act.wait_ge(tile_done, h * 2 + n0 + 1)
                        f(qh[:, e, half, :], ps[:, n0 % BANKS, :], ACT.Copy).then_inc(bank_free[n0 % BANKS], 1)
                    act.wait_ge(sc_done, h + e + 1)
                    act.wait_ge(sc_free, h + e + 1)
                    for c in range(2):
                        i = f(sc[:, e, 4 * c:4 * c + 4, :].rearrange("p r n -> p (r n)"), ps[:, 4 + c, :], ACT.Copy)
                    i.then_inc(sc_ready, 1)
                    act.wait_ge(side_done, h + e + 3)
                    act.wait_ge(h_saved[e], h2 * 16 + 16)
                    f(n_tok[:, e * T:(e + 1) * T], ps[:, 6 + e, :], ACT.Copy).then_inc(side_free, 1)
                    act.wait_ge(side_free, h + e + 3)
                    act.dma_start(hsave[:, bass.ds((h + e) * T, T)], n_tok[:, e * T:(e + 1) * T]).then_inc(h_saved[e], 16)

            for half in range(2):
                act.wait_ge(side_done, 3 + 2 * TB + half)
                act.wait_ge(h_saved[half], 16 * (TB + 1))
                f(n_tok[:, half * T:(half + 1) * T], ps[:, 6 + half, :], ACT.Copy).then_inc(side_free, 1)

            act.wait_ge(sm_in, 1)
            f(gw[:, :, :, :], gw[:, :, :, :], ACT.Exp).then_inc(sm_exp, 1)
            for q in range(3):
                n = N_LIST + q
                act.wait_ge(tile_done, n + 1)
                f(lists[:, q, :], ps[:, n % BANKS, 0:DT], ACT.Copy).then_inc(bank_free[n % BANKS], 1)

            def round_u(n, e, g):
                act.wait_ge(u_here[e], g * 16 + 16)
                act.wait_ge(u_done, n + 1)
                f(Us[:, e, 0, :], uraw[:, e, :], ACT.Copy).then_inc(uhi_ready, 1)

            act.wait_ge(xlo_ready, KT)
            nc.scalar.sem_inc(u_done, 2)
            nc.scalar.sem_inc(gel_ready, 2)
            round_u(0, 0, 0)
            nc.scalar.sem_inc(g_taken, 4)
            for k in range(PRING):
                nc.scalar.sem_inc(piece_out[k], 16)
            with act.Fori(0, PIECES // PRING) as it:
                for i in range(24):
                    c, k = i % 4, i // 8
                    if c == 0:
                        x = ohj_side[:, i // 4 % 3]
                        act.wait_ge(diff_ready, it * 6 + i // 4 + 1)
                        f(x, x, ACT.Square).then_inc(squared, 1)
                        act.wait_ge(squared, it * 6 + i // 4 + 1)
                        f(x, x, ACT.Relu, scale=-1.0, bias=ones[:, 0:1]).then_inc(ohj_ready, 1)
                    if i % 6 == 1:
                        j = i // 6
                        round_u(it * 4 + (j + 1), (j + 1) % 2, it * 2 + (j + 1) // 2)
                    if i % 8 == 0:
                        act.wait_ge(piece_out[k], it * 16 + 16)
                    act.wait_ge(oh_used, it * 24 + (i + 1 + 12))
                    f(piece[:, k, :, i % 8 * 4:i % 8 * 4 + 4].rearrange("p i t -> p t i"),
                      ps[:, c, :].rearrange("p (t i) -> p t i", t=4), ACT.Copy).then_inc(g_taken, 1)
                    if i % 6 == 2:
                        j = i // 6
                        act.wait_ge(u_done, it * 4 + (j + 1 + 2))
                        f(early[:, bass.ds(it * 4 + j, 1), :].rearrange("p a t -> p (a t)"), ps[:, 6 + j % 2, 0:DT],
                          ACT.Gelu).then_inc(gel_ready, 1)

            nc.scalar.sem_inc(ulo_ready, 1)
            nc.scalar.sem_inc(alo_ready, 3)
            nc.scalar.sem_inc(v_done, 2)
            nc.scalar.sem_inc(vlo_ready, 4)
            nc.scalar.sem_inc(a_ready, 8)

            def dense_turn(g, last=False):
                for d in range(BODY):
                    o = g * BODY + d
                    nxt = d + 1
                    if nxt % 8 != 7 and not (last and nxt == BODY):
                        i = nxt - nxt // 8
                        round_u(g * LATE + (EARLY + i), i % 2, g * (LATE // 2) + (EARLY + i) // 2)
                    if d % 8 != 7:
                        i = d - d // 8
                        act.wait_ge(u_done, g * LATE + (EARLY + i + 1 + 2))
                        before = 3 if d % 8 < 2 else 2
                        act.wait_ge(alo_ready, o + (1 + 3 - before))
                        f(gel[:, i % 2, :], ps[:, 6 + i % 2, 0:DT], ACT.Gelu).then_inc(gel_ready, 1)
                    act.wait_ge(v_here[d // 2 % 2], g * (BODY * 4) + (d // 4 + 1) * 16)
                    act.wait_ge(v_done, o + 1)
                    f(Vs[:, d % 2, 0, :], vraw[:, d // 2 % 2, d % 2, :], ACT.Copy).then_inc(vhi_ready, 1)

            with act.Fori(0, TURNS // 2) as g:
                dense_turn(g)
            act.wait_ge(dots_ready, SLOTS // ROWBUF)
            f(act_w[:, :], dots[:, :], ACT.Gelu).then_inc(gelu_ready, 1)
            with act.Fori(TURNS // 2, TURNS - 1) as g:
                dense_turn(g)
            dense_turn(TURNS - 1, True)

            for b in range(TB):
                act.wait_ge(y_sum, b + 1)
                f(row[:, 0, :], yout[:, b, :], ACT.Square, accum_out=ssum[:, b:b + 1]).then_inc(y_sq, 1)
                act.wait_ge(y_sq, b + 1)
                f(sstd[:, b:b + 1], ssum[:, b:b + 1], ACT.Sqrt, bias=eps[:, 0:1], scale=1.0 / D).then_inc(y_std, 1)

        @block.vector
        def _(dve):
            v = nc.vector
            count = [0]

            def step(ins):
                count[0] += 1
                ins.then_inc(dve_step, 1)

            def settled():
                dve.wait_ge(dve_step, count[0])

            def scale_rows(stage, between=None):
                n = N_RMS2 if stage else N_RMS1
                freed(dve, n)
                step(v.reciprocal(rstd, std))
                settled()
                for k in range(KT):
                    if stage and k == 0:
                        dve.wait_ge(gate_done, 2 * KT)
                    v.tensor_tensor(nT[:, k, :], hT[:, k, :], rstd, ALU.mult).then_inc(scaled, 1)
                    if between and k == 3:
                        between()

            def take_mod(done, c0, c1):
                dve.wait_ge(mod_done, done)
                return v.tensor_tensor(mod[:, c0:c1], (MOD if done == 1 else MOD2)[:, c0:c1], b_ada[:, c0:c1], ALU.add)

            dve.wait_ge(cond_ready, 1)

            def modulation(q):
                for k in range(KT):
                    dve.wait_ge(ada_here[k % 4], 16 * (2 * q + k // 4 + 1))
                    if k == 0:
                        i = v.tensor_scalar(macc[:, q, :], aring[:, k % 4, :], cond[:, k:k + 1], None, ALU.mult)
                    else:
                        dve.wait_ge(ada_used, q * KT + k)
                        i = v.scalar_tensor_tensor(macc[:, q, :], aring[:, k % 4, :], cond[:, k:k + 1],
                                                   macc[:, q, :], ALU.mult, ALU.add)
                    if k < KT - 1:
                        i.then_inc(ada_used, 1)
                    else:
                        i.then_inc(macc_ready, 1)
                        dve.wait_ge(macc_ready, q + 1)
                        v.sem_inc(ada_used, 1)

            def first_coefficients():
                step(take_mod(1, 0, 2 * KT))
                settled()
                v.scalar_tensor_tensor(coef[:, 0, :], mod[:, KT:2 * KT], 1.0, g1, ALU.add, ALU.mult
                                       ).then_inc(mod_ready, 1)

            modulation(0)
            modulation(1)
            dve.wait_ge(x_here, 16)
            scale_rows(0, first_coefficients)

            dve.wait_ge(consts, 4)
            for m in range(CT):
                modulation(m + 2)
                n = N_CONV + 2 * m
                dve.wait_ge(tile_done, n + 1)
                freed(dve, n + 1)
                v.tensor_tensor(u[:, m, TAPS - 1:PADT], ps[:, n % BANKS, :], sg[:, m % 2, :], ALU.mult
                                ).then_inc(bank_free[n % BANKS], 1)

            dve.wait_ge(late_here, 64)
            step(v.tensor_scalar(nsink[:, :], rowv[:, 0:HEADS], -1.0, None, ALU.mult))
            settled()

            def att_norm(a):
                c0 = P if a < PAIRS else 0
                dve.wait_ge(exp_done, a + 1)
                step(v.tensor_tensor(den[:, a % 2, :], rs[:, a % 2, :], es[:, a % 2, :], ALU.add))
                settled()
                step(v.reciprocal(rden[:, a % 2, :], den[:, a % 2, :]))
                settled()
                for e in range(2):
                    i = v.tensor_scalar(pexp[:, a % 2, e, c0:KEYS], pexp[:, a % 2, e, c0:KEYS],
                                        rden[:, a % 2, e:e + 1], None, ALU.mult)
                i.then_inc(p_ready, 1)

            tap_end = [0] * CT

            def conv_tap(k):
                for m in range(CT):
                    if k == 0:
                        i = v.tensor_scalar(y[:, m, :], u[:, m, 0:T], w_dw[:, m, 0:1], b_dw[:, m:m + 1],
                                            ALU.mult, ALU.add)
                    else:
                        dve.wait_ge(dve_step, tap_end[m])
                        i = v.scalar_tensor_tensor(y[:, m, :], u[:, m, k:k + T], w_dw[:, m, k:k + 1], y[:, m, :],
                                                   ALU.mult, ALU.add)
                    if k < TAPS - 1:
                        step(i)
                        tap_end[m] = count[0]
                    else:
                        i.then_inc(y_ready, 1)

            for k in range(TAPS_BEFORE):
                conv_tap(k)

            for a in range(TB * PAIRS):
                m = a % PAIRS
                c0 = P if a < PAIRS else 0
                S = ps[:, 2 * (a % 2):2 * (a % 2) + 2, :]
                dve.wait_ge(s_done, a + 1)
                if a >= 2:
                    dve.wait_ge(exp_done, a - 1)
                v.tensor_tensor(ssb[:, a % 2, :, c0:KEYS], S[:, :, c0:KEYS], bias[:, 2 * m:2 * m + 2, c0:KEYS],
                                ALU.add).then_inc(s_biased, 1)
                dve.wait_ge(s_biased, a + 1)
                step(v.tensor_reduce(mx[:, a % 2, :], ssb[:, a % 2, :, c0:KEYS], axis=AX.X, op=ALU.max))
                settled()
                step(v.scalar_tensor_tensor(nmx[:, a % 2, :], mx[:, a % 2, :], -1.0, nsink[:, 2 * m:2 * m + 2],
                                            ALU.mult, ALU.min))
                settled()
                v.tensor_tensor(mx[:, a % 2, :], nmx[:, a % 2, :], nsink[:, 2 * m:2 * m + 2], ALU.subtract
                                ).then_inc(nmx_ready, 1)
                if a >= 1:
                    att_norm(a - 1)
                late = TAPS - TAPS_BEFORE
                for k in range(a * late // (TB * PAIRS), (a + 1) * late // (TB * PAIRS)):
                    conv_tap(TAPS_BEFORE + k)
                if a == TB * PAIRS - 1:
                    take_mod(2, 2 * KT, 6 * KT).then_inc(mod_ready, 1)
                    dve.wait_ge(mod_ready, 2)
                    v.scalar_tensor_tensor(coef[:, 1, :], mod[:, 4 * KT:5 * KT], 1.0, g2, ALU.add, ALU.mult
                                           ).then_inc(mod_ready, 1)
            att_norm(TB * PAIRS - 1)

            dve.wait_ge(y_ready, CT)
            dve.wait_ge(tile_done, N_LN + 1)
            v.tensor_scalar(rstd, ps[:, N_LN % BANKS, :], 1.0 / (CT * P), None, ALU.mult
                            ).then_inc(bank_free[N_LN % BANKS], 1)
            freed(dve, N_LN)
            for m in range(CT):
                v.tensor_tensor(y[:, m, :], y[:, m, :], rstd, ALU.subtract).then_inc(yc_ready, 1)
            freed(dve, N_LN + 1)
            step(v.reciprocal(rstd, std))
            settled()
            dve.wait_ge(yc_ready, CT)
            for m in range(CT):
                v.tensor_tensor(y[:, m, :], y[:, m, :], rstd, ALU.mult).then_inc(yn_ready, 1)

            def merged_rest(d):
                dve.wait_ge(merged_hi, d + 1)
                v.tensor_tensor(mparts[:, 1, d, :], gates[:, d, :], mparts[:, 0, d, :].bitcast(f32), ALU.subtract
                                ).then_inc(merged_lo, 1)

            def wout_rest(d):
                dve.wait_ge(wout_hi, d + 1)
                v.tensor_tensor(wparts[:, d % 2, 1, :], wring[:, d // 2, d % 2, :, :].rearrange("p k c -> p (k c)"),
                                wparts[:, d % 2, 0, :].bitcast(f32), ALU.subtract).then_inc(wout_lo, 1)

            for d in range(KT):
                n = N_PROJ + (d if d < 4 else 2 * d - 4)
                if d % 4 == 0:
                    dve.wait_ge(gates_ready, 2 * (d // 4) + 2)
                if d < 4:
                    dve.wait_ge(attn_projected, d + 1)
                dve.wait_ge(tile_done, n + (1 if d < 4 else 2))
                v.tensor_tensor(gates[:, d, :], ps[:, n % BANKS, :], gates[:, d, :], ALU.mult
                                ).then_inc(bank_free[n % BANKS], 1)
                if d < 4:
                    v.tensor_tensor(gates[:, KT + d, :], ps[:, 4 + d, :], gates[:, KT + d, :], ALU.mult
                                    ).then_inc(attn_merged, 1)
                    dve.wait_ge(attn_merged, d + 1)
                else:
                    v.tensor_tensor(gates[:, KT + d, :], ps[:, (n + 1) % BANKS, :], gates[:, KT + d, :], ALU.mult
                                    ).then_inc(bank_free[(n + 1) % BANKS], 1)
                    freed(dve, n + 1)
                freed(dve, n)
                v.tensor_tensor(gates[:, d, :], gates[:, d, :], gates[:, KT + d, :], ALU.add).then_inc(merged, 1)
                if d >= 1:
                    merged_rest(d - 1)
                if d == 5:
                    wout_rest(0)
                    wout_rest(1)
            merged_rest(KT - 1)

            dve.wait_ge(mod_ready, 2)
            for d in range(KT):
                n = N_WOUT + d
                dve.wait_ge(tile_done, n + 1)
                v.scalar_tensor_tensor(hT[:, d, :], ps[:, n % BANKS, :], mod[:, 2 * KT + d:2 * KT + d + 1], hT[:, d, :],
                                       ALU.mult, ALU.add).then_inc(bank_free[n % BANKS], 1)
                if d + 2 < KT:
                    wout_rest(d + 2)
            for k in range(4, KT):
                freed(dve, N_WOUT + k)
            scale_rows(1)

            for k in range(KT):
                i = v.tensor_scalar(diag[:, k, :], ident[:, :], mod[:, 5 * KT + k:5 * KT + k + 1], None, ALU.mult)
            i.then_inc(mod_ready, 1)

            step(v.memset(c15, 15))
            base = count[0]
            per = [0]

            def hstep(ins, h):
                per[0] += 1
                ins.then_inc(dve_step, 1)

            def hsettled(h, e, k):
                dve.wait_ge(dve_step, h * k + base + per[0])
                v.sem_inc(dve_turn, 1)

            STEPS = 72
            def one_hot(h):
                dve.wait_ge(sel_free, h + 1)
                for half in range(2):
                    i = v.tensor_tensor(hot[:, half].rearrange("p b k a -> p (b k) a"),
                                        posa[:, half].rearrange("p b k -> p (b k)").unsqueeze(2)
                                        .broadcast_to([P, TB * TOPK, TOPK]),
                                        iotan[:, 1 - half:1 - half + TOPK].unsqueeze(1)
                                        .broadcast_to([P, TB * TOPK, TOPK]), ALU.is_equal)
                i.then_inc(pos_ready, 1)

            def two_heads(h2, last=False):
                h = h2 * 2
                per[0] = 0
                for e in range(2):
                    start = per[0]
                    dve.wait_ge(sc_ready, h + e + 2)
                    v.sem_inc(dve_turn, 1)
                    for b in range(TB):
                        for half in range(2):
                            hstep(v.max(vals[:, b, half, 0:8], sc[:, e, 2 * b + half, :]), h)
                    hsettled(h, e, STEPS)
                    for b in range(TB):
                        for half in range(2):
                            hstep(v.match_replace(out=sc2[:, 2 * b + half, :], in_to_replace=vals[:, b, half, 0:8],
                                                  in_values=sc[:, e, 2 * b + half, :], imm_value=NEG), h)
                            hstep(v.max_index(out=vidx[:, b, half, 0:8], in_max=vals[:, b, half, 0:8],
                                              in_values=sc[:, e, 2 * b + half, :]), h)
                    hsettled(h, e, STEPS)
                    for b in range(TB):
                        for half in range(2):
                            hstep(v.max(vals[:, b, half, 8:16], sc2[:, 2 * b + half, :]), h)
                    hsettled(h, e, STEPS)
                    for b in range(TB):
                        for half in range(2):
                            i = v.max_index(out=vidx[:, b, half, 8:16], in_max=vals[:, b, half, 8:16],
                                            in_values=sc2[:, 2 * b + half, :])
                            hstep(i, h)
                    for s in range(5):
                        na, nb = min(1 << s, TOPK - (1 << s) + 1), TOPK >> s
                        a0 = (1 << s) - 1
                        hstep(v.tensor_tensor(
                            cand[:, :, 16 * s:16 * s + na * nb].rearrange("p t (a b) -> p t a b", a=na),
                            vals[:, :, 0, a0:a0 + na].unsqueeze(3).broadcast_to([P, TB, na, nb]),
                            vals[:, :, 1, 0:nb].unsqueeze(2).broadcast_to([P, TB, na, nb]), ALU.add), h)
                    hsettled(h, e, STEPS)
                    v.tensor_copy(vidf[e], vidx).then_inc(sc_free, 1)
                    for b in range(TB):
                        hstep(v.max(best[:, b, 0:8], cand[:, b, :]), h)
                    hsettled(h, e, STEPS)
                    for b in range(TB):
                        hstep(v.match_replace(out=cand2[:, b, :], in_to_replace=best[:, b, 0:8],
                                              in_values=cand[:, b, :], imm_value=NEG), h)
                        hstep(v.max_index(out=pos[:, b, 0:8], in_max=best[:, b, 0:8], in_values=cand[:, b, :]), h)
                    hsettled(h, e, STEPS)
                    for b in range(TB):
                        hstep(v.max(best[:, b, 8:16], cand2[:, b, :]), h)
                    hsettled(h, e, STEPS)
                    for b in range(TB):
                        hstep(v.max_index(out=pos[:, b, 8:16], in_max=best[:, b, 8:16], in_values=cand2[:, b, :]), h)
                    hstep(v.tensor_copy(bests[:, :, bass.ds(h + e, 1), :].rearrange("p b a k -> p b (a k)"),
                                        best[:, :, :]), h)
                    hsettled(h, e, STEPS)
                    hstep(v.tensor_scalar(seg, pos, 4, None, ALU.logical_shift_right), h)
                    hstep(v.tensor_scalar(low4, pos, 15, 16, ALU.bitwise_and, ALU.bitwise_or), h)
                    hsettled(h, e, STEPS)
                    hstep(v.tensor_scalar(sh, seg, -1.0, 4.0, ALU.mult, ALU.add), h)
                    hstep(v.tensor_tensor(mask, c15, seg, ALU.logical_shift_right), h)
                    hsettled(h, e, STEPS)
                    hstep(v.tensor_tensor(posa[:, 0], low4, sh, ALU.logical_shift_right), h)
                    hstep(v.tensor_tensor(posa[:, 1], pos, mask, ALU.bitwise_and), h)
                    hsettled(h, e, STEPS)
                    if not (last and e == 1):
                        one_hot(h + e)
                assert per[0] == 2 * STEPS, per

            with dve.Fori(0, PH // 2 - 1) as h2:
                two_heads(h2)
            two_heads(PH // 2 - 1, True)
            count[0] = base + PH * STEPS

            v.tensor_tensor(gw, bests, bests[:, :, :, 0:1].broadcast_to([P, TB, PH, TOPK]), ALU.subtract
                            ).then_inc(sm_in, 1)
            one_hot(PH - 1)
            dve.wait_ge(pos_ready, PH)
            for half in range(2):
                step(v.tensor_tensor(hot[:, half], hot[:, half], vidf[1][:, :, half, :].unsqueeze(2)
                                     .broadcast_to([P, TB, TOPK, TOPK]), ALU.mult))
            settled()
            for half, dst in enumerate((isel, jsel)):
                step(v.tensor_reduce(dst[:, :, PH - 1, :], hot[:, half], axis=AX.X, op=ALU.add))
            dve.wait_ge(sm_exp, 1)
            gv = gw.rearrange("p b h k -> p (b h) k")
            step(v.tensor_reduce(gsum[:, :], gv, axis=AX.X, op=ALU.add))
            settled()
            step(v.reciprocal(gsum[:, :], gsum[:, :]))
            settled()
            dve.wait_ge(sel_free, PH)
            v.tensor_tensor(gv, gv, gsum[:, :].unsqueeze(2).broadcast_to([P, TB * PH, TOPK]), ALU.mult
                            ).then_inc(list_in, 1)
            v.scalar_tensor_tensor(eidx[:, :], isel[:, 0, :, :].rearrange("p h k -> p (h k)"), float(NK),
                                   jsel[:, 0, :, :].rearrange("p h k -> p (h k)"), ALU.mult, ALU.add
                                   ).then_inc(idx_ready, 1)

            for q in range(3):
                freed(dve, N_LIST + q)
            with dve.Fori(0, DT // 16) as it:
                for c in range(4):
                    dve.wait_ge(oh_used, it * 4 + (c + 1 + 8))
                    if c < 3:
                        v.tensor_tensor(ohj[:, 4 * c:4 * c + 4, :], iotan[:, :].unsqueeze(1).broadcast_to([P, 4, NK]),
                                        lists[:, 1, bass.ds(it * 16 + 4 * c, 4)].unsqueeze(2).broadcast_to([P, 4, NK]),
                                        ALU.is_equal)
                    for t in range(4):
                        tok = it * 16 + 4 * c + t
                        i = v.tensor_scalar(ohi[:, 4 * c + t, :], iotan[:, :], lists[:, 0, bass.ds(tok, 1)],
                                            lists[:, 2, bass.ds(tok, 1)], ALU.is_equal, ALU.mult)
                    i.then_inc(oh_ready, 1)

            def rest_u(n, e):
                dve.wait_ge(uhi_ready, n + 1)
                v.tensor_tensor(Us[:, e, 1, :], uraw[:, e, :], Us[:, e, 0, :].bitcast(f32), ALU.subtract
                                ).then_inc(ulo_ready, 1)

            def weigh(g, d):
                o, a = g * BODY + d, d % 2
                if d % 8 == 7:
                    act_t = early[:, bass.ds(g * 2 + d // 8, 1), :].rearrange("p a t -> p (a t)")
                else:
                    i = d - d // 8
                    dve.wait_ge(gel_ready, g * LATE + (EARLY + i + 1 + 2))
                    act_t = gel[:, i % 2, :]
                dve.wait_ge(g_here[d // 4 % 2], g * 32 + (d // 8 + 1) * 16)
                ga = act_t.rearrange("p (h t) -> p h t", h=PIECES)
                v.tensor_tensor(ga, ga, graw[:, d // 4 % 2, :, d % 4, :], ALU.mult).then_inc(a_ready, 1)
                dve.wait_ge(v_done, o + 1)
                dve.wait_ge(a_ready, o + (1 + 8))
                v.sem_inc(dve_turn, 1)
                v.tensor_copy(As[:, a, 0, :], act_t).then_inc(ahi_ready, 1)
                dve.wait_ge(ahi_ready, o + 1)
                v.tensor_tensor(As[:, a, 1, :], act_t, As[:, a, 0, :].bitcast(f32), ALU.subtract
                                ).then_inc(alo_ready, 1)
                dve.wait_ge(vhi_ready, o + 1)
                v.tensor_tensor(Vs[:, a, 1, :], vraw[:, d // 2 % 2, d % 2, :], Vs[:, a, 0, :].bitcast(f32), ALU.subtract
                                ).then_inc(vlo_ready, 1)

            def dot(g, s):
                dve.wait_ge(row_here[s], (g + 1) * 16)
                v.tensor_tensor_reduce(out=row[:, s, :], in0=row[:, s, :], in1=n_tok, scale=1.0, scalar=0.0,
                                       op0=ALU.mult, op1=ALU.add, accum_out=dot1[:, s:s + 1]).then_inc(row_used, 1)

            def dots_out(g):
                dve.wait_ge(row_used, g * ROWBUF + ROWBUF)
                v.tensor_copy(dots[:, bass.ds(g * ROWBUF, ROWBUF)], dot1[:, :]).then_inc(dots_ready, 1)
                dve.wait_ge(dots_ready, g + 1)

            def add_row(g, s):
                dve.wait_ge(row_here[s], (g + 1) * 16)
                dve.wait_ge(row_used, g * ROWBUF + (s - 1))
                v.scalar_tensor_tensor(acc[:, s % 2, :], row[:, s, :],
                                       act_w[:, bass.ds(g * ROWBUF + (s - SLOTS), 1)],
                                       acc[:, s % 2, :], ALU.mult, ALU.add).then_inc(row_used, 1)

            def dense_turn(g, rows, last=False):
                for d in range(BODY):
                    nxt = d + 1
                    if nxt % 8 != 7 and not (last and nxt == BODY):
                        i = nxt - nxt // 8
                        rest_u(g * LATE + (EARLY + i), i % 2)
                    weigh(g, d)
                    for s in (2 * (d % 4), 2 * (d % 4) + 1):
                        rows(g * 4 + d // 4, s)
                    if rows is dot and d % 4 == 3:
                        dots_out(g * 4 + d // 4)

            with dve.Fori(0, TURNS // 2) as g:
                dense_turn(g, dot)
            step(v.memset(acc[:, 0, :], 0.0))
            step(v.memset(acc[:, 1, :], 0.0))
            dve.wait_ge(gelu_ready, 1)
            step(v.tensor_tensor(act_w[:, :], act_w[:, :], gw[:, 0, :, :].rearrange("p h k -> p (h k)"), ALU.mult))
            settled()
            with dve.Fori(TURNS // 2, TURNS - 1) as g:
                dense_turn(g, add_row)
            dense_turn(TURNS - 1, add_row, True)
            dve.wait_ge(row_used, 2 * SLOTS)
            step(v.tensor_tensor(acc[:, 0, :], acc[:, 0, :], acc[:, 1, :], ALU.add))
            settled()

            dve.wait_ge(h_here, 16)
            def residual(b):
                if b >= 1:
                    dve.wait_ge(v_done, XT + 1 + b)
                src = acc[:, 0, :] if b == 0 else ps[:, 2 * b - 2:2 * b, :].rearrange("p h d -> p (h d)")
                step(v.tensor_tensor(yout[:, b, :], src, g2row, ALU.mult))
                settled()
                v.tensor_tensor(yout[:, b, :], yout[:, b, :], h_tok[:, b, :], ALU.add).then_inc(y_sum, 1)

            def norm(b):
                dve.wait_ge(y_std, b + 1)
                step(v.reciprocal(srstd[:, b:b + 1], sstd[:, b:b + 1]))
                settled()
                v.scalar_tensor_tensor(yout[:, b, :], yout[:, b, :], srstd[:, b:b + 1], gfin, ALU.mult, ALU.mult
                                       ).then_inc(y_out, 1)

            residual(0)
            norm(0)
            residual(1)
            for b in range(2, TB):
                residual(b)
                norm(b - 1)
            norm(TB - 1)


def slope_bias():
    slopes = (2.0 ** (-8.0 * np.arange(1, HEADS + 1) / HEADS)).astype(np.float32)
    q = np.arange(P)[:, None] + P
    k = np.arange(KEYS)[None, :]
    chunk = k // HD - q // HD
    seen = (chunk == 0) | (chunk == -1)
    dist = np.abs(q - k).astype(np.float32)
    order = [m + PAIRS * e for m in range(PAIRS) for e in range(2)]
    return np.stack([np.where(seen, -slopes[h] * dist, np.float32(-1e30)) for h in order], 1).astype(np.float32)


def tiles(w):
    n = w.shape[1] // P
    return w.reshape(-1, P, n, P).transpose(2, 1, 0, 3).reshape(n, P, -1)


def kernel(x, c, w_ada, b_ada, g_norm1, w_in, w_dw, b_dw, ln_g, ln_b, w_conv_out, w_attn_out, attn_sinks, w_out,
           g_norm2, w_pq, sub_keys, peer_u, peer_v, g_final):
    import concourse.bacc as _bacc
    from concourse import mybir as _mybir
    from concourse.bass_utils import run_bass_kernel_spmd as _run

    A = np.asarray
    w_in = A(w_in)[0]
    pair = [m + PAIRS * e for m in range(PAIRS) for e in range(2)]
    w_q = w_in[:, 1024:1536].reshape(D, HEADS, HD)[:, pair].reshape(D, -1)
    w_ao = A(w_attn_out)[0].reshape(HEADS, HD, D)[pair].reshape(-1, D)
    conv = tiles(w_in[:, 0:1024])[[0, 4, 1, 5, 2, 6, 3, 7]]
    stream = np.concatenate([conv, tiles(w_in[:, 1792:3840]), tiles(np.concatenate([A(w_conv_out)[0], w_ao])),
                             tiles(A(w_out)[0]), tiles(A(w_pq)[0])])
    stream = np.ascontiguousarray(stream.reshape(ROUNDS * 4, 2, P, -1).transpose(0, 2, 1, 3).reshape(ROUNDS * 4, P, -1))
    wqkv = tiles(np.concatenate([w_q, w_in[:, 1536:1792]], 1)).transpose(1, 0, 2).reshape(P, -1)
    col = lambda a: A(a).reshape(-1, P).T
    cols = np.concatenate([col(b_ada), col(g_norm1), col(g_norm2), col(b_dw), col(ln_g), col(ln_b),
                           A(w_dw)[0].T.reshape(CT, P, TAPS).transpose(1, 0, 2).reshape(P, -1), col(c)], 1)
    rows = np.broadcast_to(np.concatenate([A(attn_sinks)[0][pair], A(g_final)])[None], (P, HEADS + D))
    hidden_order = [n for n in range(XT) if n % 8 == 7] + [n for n in range(XT) if n % 8 != 7]
    arrays = {
        "stream": stream, "wada": A(w_ada)[0].reshape(KT, P, MODS, D).transpose(2, 0, 1, 3).reshape(MODS * KT, P, D),
        "wqkv": wqkv,
        "skT": A(sub_keys)[0].reshape(2 * PH, NK, P).transpose(2, 0, 1),
        "xT": A(x)[0].T.reshape(KT, P, T).transpose(1, 0, 2),
        "cols": cols, "rows": rows, "biasd": slope_bias(), "identd": np.eye(P, dtype=np.float32),
        "puT": tiles(A(peer_u)[0].T)[hidden_order],
        "pu": A(peer_u)[0], "pv": A(peer_v)[0],
    }
    arrays = {k: np.ascontiguousarray(a) for k, a in arrays.items()}
    nc = _bacc.Bacc("TRN2", target_bir_lowering=False, num_devices=1)
    aps = [nc.dram_tensor(k, a.shape, _mybir.dt.from_np(a.dtype), kind="ExternalInput").ap() for k, a in arrays.items()]
    out = nc.dram_tensor("out", (T, D), _mybir.dt.float32, kind="ExternalOutput").ap()
    gmat = nc.dram_tensor("gmat", (PIECES, P, NK * HT), _mybir.dt.float32, kind="Internal").ap()
    hsave = nc.dram_tensor("hsave", (P, TB * D), _mybir.dt.float32, kind="Internal").ap()
    build(nc, *aps, gmat, hsave, out)
    r = _run(nc, [arrays], core_ids=[0])
    return r.results[0]["out"].reshape(1, T, D)
```
